# Optimizing a Trainium2 kernel written in Bass

```python
import jax, jax.numpy as jnp
from jax import lax
import numpy as np

D_MODEL = 1024
BATCH = 1
SEQ = 256
DEPTH = 1

GRID_W = 64
N_META = 16
EPS = 1e-6

NA_HEADS = 8
NA_HEAD_DIM = 64
NA_WIDTH = NA_HEADS * NA_HEAD_DIM
NA_WIN_H = 8
NA_WIN_W = 16

HG_HEADS = 4
HG_DK = 128
HG_DV = 128
HG_KDIM = HG_HEADS * HG_DK
HG_VDIM = HG_HEADS * HG_DV
HG_CHUNK = 16

D_FF = 4 * D_MODEL

IN_SPLIT = (NA_WIDTH, NA_WIDTH, NA_WIDTH,
            HG_KDIM, HG_KDIM, HG_KDIM, HG_VDIM, HG_VDIM,
            D_MODEL, D_MODEL)
IN_COLS = sum(IN_SPLIT)


def rms_norm(x, g):
    xf = x.astype(jnp.float32)
    y = xf * lax.rsqrt(jnp.mean(xf * xf, axis=-1, keepdims=True) + EPS)
    return (y * g.astype(jnp.float32)).astype(x.dtype)

def split_cols(a):
    outs, off = [], 0
    for n in IN_SPLIT:
        outs.append(a[..., off:off + n])
        off += n
    return outs

def neighbourhood_attention(q, k, v, rpb):
    B, L, H, dh = q.shape
    T = L - N_META
    rows = T // GRID_W
    kh = min(NA_WIN_H, rows)
    scale = dh ** -0.5
    qm, km, vm = q[:, :N_META], k[:, :N_META], v[:, :N_META]
    qg = q[:, N_META:].reshape(B, rows, GRID_W, H, dh)
    kg = k[:, N_META:].reshape(B, rows, GRID_W, H, dh)
    vg = v[:, N_META:].reshape(B, rows, GRID_W, H, dh)

    r = jnp.arange(rows)
    row_start = jnp.clip(r - kh // 2, 0, rows - kh)
    row_idx = row_start[:, None] + jnp.arange(kh)[None, :]
    k_blk = kg[:, row_idx]
    v_blk = vg[:, row_idx]

    s_win = jnp.einsum('brchd,brjwhd->bhrcjw', qg, k_blk).astype(jnp.float32) * scale
    c = jnp.arange(GRID_W)
    col_start = jnp.clip(c - NA_WIN_W // 2, 0, GRID_W - NA_WIN_W)
    in_win = (c[None, :] >= col_start[:, None]) & (c[None, :] < col_start[:, None] + NA_WIN_W)
    dr = row_idx - r[:, None]
    dc = jnp.clip(c[None, :] - c[:, None], -(NA_WIN_W - 1), NA_WIN_W - 1)
    bias = rpb.astype(jnp.float32)[:, dr[:, None, :, None] + NA_WIN_H - 1,
                                   dc[None, :, None, :] + NA_WIN_W - 1]
    s_win = jnp.where(in_win[:, None, :], s_win + bias[None], -1e30)

    s_meta = jnp.einsum('brchd,bmhd->bhrcm', qg, km).astype(jnp.float32) * scale
    s = jnp.concatenate([s_win.reshape(B, H, rows, GRID_W, kh * GRID_W), s_meta], axis=-1)
    p = jax.nn.softmax(s, axis=-1).astype(v.dtype)
    p_win = p[..., :kh * GRID_W].reshape(B, H, rows, GRID_W, kh, GRID_W)
    p_meta = p[..., kh * GRID_W:]
    o_grid = (jnp.einsum('bhrcjw,brjwhd->brchd', p_win, v_blk)
              + jnp.einsum('bhrcm,bmhd->brchd', p_meta, vm)).reshape(B, T, H, dh)

    s_mm = jnp.einsum('bmhd,bnhd->bhmn', qm, km).astype(jnp.float32) * scale
    p_mm = jax.nn.softmax(s_mm, axis=-1).astype(v.dtype)
    o_meta = jnp.einsum('bhmn,bnhd->bmhd', p_mm, vm)
    return jnp.concatenate([o_meta, o_grid], axis=1)

def chunk_scan(q, k, v, log_f):
    B, L, H, dk = q.shape
    dv = v.shape[-1]
    n = L // HG_CHUNK

    def to_chunks(a):
        return a.reshape(B, n, HG_CHUNK, H, a.shape[-1]).transpose(1, 0, 3, 2, 4)

    tri = jnp.tril(jnp.ones((HG_CHUNK, HG_CHUNK), dtype=bool))

    def step(S, inp):
        qi, ki, vi, gi = inp
        b = jnp.cumsum(gi, axis=-2)
        o_inter = jnp.einsum('bhtk,bhkv->bhtv', qi * jnp.exp(b), S)
        diff = jnp.where(tri[:, :, None], b[..., :, None, :] - b[..., None, :, :], -jnp.inf)
        A = jnp.einsum('bhtk,bhsk,bhtsk->bhts', qi, ki, jnp.exp(diff))
        o_intra = jnp.einsum('bhts,bhsv->bhtv', A, vi)
        b_last = b[..., -1:, :]
        S_new = (jnp.exp(b_last[..., 0, :])[..., None] * S
                 + jnp.einsum('bhsk,bhsv->bhkv', ki * jnp.exp(b_last - b), vi))
        return S_new, o_inter + o_intra

    S0 = jnp.zeros((B, H, dk, dv), jnp.float32)
    _, o = lax.scan(step, S0, (to_chunks(q), to_chunks(k), to_chunks(v), to_chunks(log_f)))
    return o.transpose(1, 0, 3, 2, 4).reshape(B, L, H, dv)

def hgrn2_branch(q, z_fwd, z_bwd, i, g, lb, gain):
    B, L, _ = q.shape
    dtype = q.dtype

    def heads(a, d):
        return a.astype(jnp.float32).reshape(B, L, HG_HEADS, d)

    qh = jax.nn.silu(heads(q, HG_DK))
    vh = heads(i, HG_DV)

    def gates(z, lb_dir):
        lb_h = lb_dir.reshape(HG_HEADS, HG_DK)
        log_f = jnp.logaddexp(jnp.log(lb_h), jnp.log1p(-lb_h) + jax.nn.log_sigmoid(heads(z, HG_DK)))
        return -jnp.expm1(log_f), log_f

    k_f, lf_f = gates(z_fwd, lb[0])
    k_b, lf_b = gates(z_bwd, lb[1])
    rev = lambda a: jnp.flip(a, axis=1)
    o = chunk_scan(qh, k_f, vh, lf_f) + rev(chunk_scan(rev(qh), rev(k_b), rev(vh), rev(lf_b)))
    o = o * lax.rsqrt(jnp.mean(o * o, axis=-1, keepdims=True) + EPS)
    o = o.reshape(B, L, HG_VDIM) * gain.astype(jnp.float32) * jax.nn.silu(g.astype(jnp.float32))
    return o.astype(dtype)

def first_inputs(seed: int = 0) -> dict:
    key = jax.random.key(seed)
    ks = jax.random.split(key, 14)
    f32 = jnp.float32
    nrm = lambda k, shape, s: jax.random.normal(k, shape, f32) * s
    return {
        "x": nrm(ks[0], (BATCH, SEQ, D_MODEL), 1.0),
        "meta_tokens": nrm(ks[1], (N_META, D_MODEL), 1.0),
        "w_in": nrm(ks[2], (DEPTH, D_MODEL, IN_COLS), D_MODEL ** -0.5),
        "w_na_out": nrm(ks[3], (DEPTH, NA_WIDTH, D_MODEL), NA_WIDTH ** -0.5),
        "w_hg_out": nrm(ks[4], (DEPTH, HG_VDIM, D_MODEL), HG_VDIM ** -0.5),
        "w_o": nrm(ks[5], (DEPTH, D_MODEL, D_MODEL), D_MODEL ** -0.5),
        "w_up": nrm(ks[6], (DEPTH, D_MODEL, D_FF), D_MODEL ** -0.5),
        "w_down": nrm(ks[7], (DEPTH, D_FF, D_MODEL), D_FF ** -0.5),
        "norm_mix": 1.0 + nrm(ks[8], (DEPTH, D_MODEL), 0.05),
        "norm_mlp": 1.0 + nrm(ks[9], (DEPTH, D_MODEL), 0.05),
        "norm_final": 1.0 + nrm(ks[10], (D_MODEL,), 0.05),
        "hg_norm": 1.0 + nrm(ks[11], (DEPTH, HG_VDIM), 0.05),
        "na_rpb": nrm(ks[12], (DEPTH, NA_HEADS, 2 * NA_WIN_H - 1, 2 * NA_WIN_W - 1), 0.1),
        "hg_lb_logits": nrm(ks[13], (2, DEPTH + 1, HG_KDIM), 0.5),
    }

def first_block(x, meta_tokens, w_in, w_na_out, w_hg_out, w_o, w_up, w_down,
              norm_mix, norm_mlp, norm_final, hg_norm, na_rpb, hg_lb_logits):
    B = x.shape[0]
    h = jnp.concatenate([jnp.broadcast_to(meta_tokens.astype(x.dtype)[None], (B, N_META, D_MODEL)), x], axis=1)
    L = h.shape[1]
    lb_all = jnp.cumsum(jax.nn.softmax(hg_lb_logits.astype(jnp.float32), axis=1), axis=1)
    for l in range(DEPTH):
        a = rms_norm(h, norm_mix[l])
        (q_na, k_na, v_na, q_hg, z_f, z_b, i_hg, g_hg, gate_na, gate_hg) = split_cols(a @ w_in[l])
        hd = lambda t: t.reshape(B, L, NA_HEADS, NA_HEAD_DIM)
        y_na = neighbourhood_attention(hd(q_na), hd(k_na), hd(v_na), na_rpb[l]).reshape(B, L, NA_WIDTH) @ w_na_out[l]
        y_hg = hgrn2_branch(q_hg, z_f, z_b, i_hg, g_hg, lb_all[:, l], hg_norm[l]) @ w_hg_out[l]
        mix = jax.nn.sigmoid(gate_na) * y_na + jax.nn.sigmoid(gate_hg) * y_hg
        h = h + mix @ w_o[l]
        m = rms_norm(h, norm_mlp[l])
        h = h + jnp.square(jax.nn.relu(m @ w_up[l])) @ w_down[l]
    h = rms_norm(h, norm_final)
    return h[:, N_META:]


DEPTH_2 = 2

CHUNK = 64
POOL_WINDOWS = (2, 4, 8, 16)
POOL_GROUP = D_MODEL // 4
POOL_WIDTH = 4 * POOL_GROUP
SGU_LEN = 128
SGU_HEAD_DIM = 128
SGU_WIDTH = D_MODEL
SGU_HEADS = SGU_WIDTH // SGU_HEAD_DIM
GLA_HEADS = 4
GLA_KW = D_MODEL // 2
GLA_VW = D_MODEL
GLA_DK = GLA_KW // GLA_HEADS
GLA_DV = GLA_VW // GLA_HEADS
GLA_RANK = 16
GLA_TAU = 16.0
SB_HEAD_DIM = 128
SB_WIDTH = D_MODEL
SB_HEADS = SB_WIDTH // SB_HEAD_DIM
SB_QBLOCK = 128
EVEN_SIZES = (POOL_WIDTH, SGU_WIDTH, SGU_WIDTH, POOL_WIDTH + SGU_WIDTH)
ODD_SIZES = (GLA_KW, GLA_KW, GLA_VW, GLA_RANK, SB_WIDTH, SB_WIDTH, SB_WIDTH, GLA_VW + SB_WIDTH)
EVEN_IN = sum(EVEN_SIZES)
ODD_IN = sum(ODD_SIZES)
EVEN_MIX = POOL_WIDTH + SGU_WIDTH
ODD_MIX = GLA_VW + SB_WIDTH
N_EVEN = (DEPTH_2 + 1) // 2
N_ODD = DEPTH_2 // 2


def _split(t, sizes):
    idx = [int(i) for i in np.cumsum(sizes)[:-1]]
    return jnp.split(t, idx, axis=-1)

def rmsnorm(x, g):
    xf = x.astype(jnp.float32)
    y = xf * lax.rsqrt(jnp.mean(xf * xf, axis=-1, keepdims=True) + EPS)
    return (y * g.astype(jnp.float32)).astype(x.dtype)

def ada_modulate(x, c, norm_g, ada_w, ada_b):
    ada = jax.nn.silu(c) @ ada_w + ada_b
    shift, scale, gate = jnp.split(ada, 3, axis=-1)
    h = rmsnorm(x, norm_g) * (1.0 + scale[:, None, :]) + shift[:, None, :]
    return h, gate[:, None, :]

def pool_mixer(a, pool_w, pool_scale):
    B_, S, _ = a.shape
    af = a.astype(jnp.float32)
    cs = jnp.concatenate([jnp.zeros_like(af[:, :1]), jnp.cumsum(af, axis=1)], axis=1)
    t = np.arange(S)
    outs = []
    for g, w in enumerate(POOL_WINDOWS):
        sl = slice(g * POOL_GROUP, (g + 1) * POOL_GROUP)
        start = np.maximum(t + 1 - w, 0)
        count = jnp.asarray((t + 1 - start).astype(np.float32))
        win_sum = cs[:, 1:, sl] - cs[:, start, sl]
        outs.append(win_sum / count[None, :, None] - af[..., sl])
    p = jnp.stack(outs, axis=2).astype(a.dtype)
    y = jnp.einsum('bsgc,gcd->bsgd', p, pool_w).reshape(B_, S, POOL_WIDTH)
    return y * pool_scale

def spatial_gating(u, v, norm_g, w_s, b_s):
    B_, S, _ = u.shape
    n = S // SGU_LEN
    vh = rmsnorm(v, norm_g).reshape(B_, n, SGU_LEN, SGU_HEADS, SGU_HEAD_DIM)
    mask = jnp.tril(jnp.ones((SGU_LEN, SGU_LEN), dtype=bool))
    w = jnp.where(mask[None], w_s, jnp.zeros_like(w_s))
    z = jnp.einsum('hts,bnshd->bnthd', w, vh) + b_s.T[None, None, :, :, None]
    return u * z.reshape(B_, S, SGU_WIDTH)

def gla(q, k, v, log_a):
    B_, S = q.shape[:2]
    n = S // CHUNK
    r = lambda t: t.astype(jnp.float32).reshape(B_, n, CHUNK, *t.shape[2:])
    qf = r(q) * (GLA_DK ** -0.5)
    kf, vf, la = r(k), r(v), r(log_a)
    bcum = jnp.cumsum(la, axis=2)
    b_last = bcum[:, :, -1]
    q_dec = qf * jnp.exp(bcum)
    k_inv = kf * jnp.exp(-bcum)
    k_end = kf * jnp.exp(b_last[:, :, None] - bcum)
    mask = jnp.tril(jnp.ones((CHUNK, CHUNK), dtype=bool))
    att = jnp.einsum('bnthk,bnshk->bnhts', q_dec, k_inv)
    att = jnp.where(mask, att, 0.0)
    o_intra = jnp.einsum('bnhts,bnshv->bnthv', att, vf)

    def step(state, xs):
        qd, ke, vc, bl = xs
        o = jnp.einsum('bthk,bhkv->bthv', qd, state)
        state = jnp.exp(bl)[..., None] * state + jnp.einsum('bshk,bshv->bhkv', ke, vc)
        return state, o

    s0 = jnp.zeros((B_, GLA_HEADS, GLA_DK, GLA_DV), jnp.float32)
    xs = (jnp.moveaxis(q_dec, 1, 0), jnp.moveaxis(k_end, 1, 0), jnp.moveaxis(vf, 1, 0), jnp.moveaxis(b_last, 1, 0))
    _, o_inter = lax.scan(step, s0, xs)
    o = o_intra + jnp.moveaxis(o_inter, 0, 1)
    return o.reshape(B_, S, GLA_HEADS, GLA_DV).astype(v.dtype)

def stick_breaking(q, k, v):
    B_, S, H, Dh = q.shape
    scale = Dh ** -0.5
    outs = []
    for i in range(S // SB_QBLOCK):
        q0, q1 = i * SB_QBLOCK, (i + 1) * SB_QBLOCK
        z = jnp.einsum('bthd,bshd->bhts', q[:, q0:q1], k[:, :q1]).astype(jnp.float32) * scale
        strict = np.arange(q1)[None, :] < np.arange(q0, q1)[:, None]
        log_beta = jax.nn.log_sigmoid(z)
        log_1m = jnp.where(strict, jax.nn.log_sigmoid(-z), 0.0)
        after = lax.cumsum(log_1m, axis=3, reverse=True) - log_1m
        w = jnp.where(strict, jnp.exp(log_beta + after), 0.0)
        outs.append(jnp.einsum('bhts,bshd->bthd', w.astype(v.dtype), v[:, :q1]))
    return jnp.concatenate(outs, axis=1)

def even_layer(x, c, norm_g, ada_w, ada_b, in_w, pool_w, pool_scale, sgu_norm_g, sgu_w, sgu_b, out_w):
    h, gate_res = ada_modulate(x, c, norm_g, ada_w, ada_b)
    a, u, v, gate = _split(h @ in_w, EVEN_SIZES)
    ya = pool_mixer(a, pool_w, pool_scale)
    yb = spatial_gating(u, v, sgu_norm_g, sgu_w, sgu_b)
    y = jnp.concatenate([ya, yb], axis=-1) * jax.nn.silu(gate)
    return x + gate_res * (y @ out_w)

def odd_layer(x, c, norm_g, ada_w, ada_b, in_w, gate_w, gate_b, gla_norm_g, out_w):
    B_, S, _ = x.shape
    h, gate_res = ada_modulate(x, c, norm_g, ada_w, ada_b)
    gq, gk, gv, glr, sq, sk, sv, gate = _split(h @ in_w, ODD_SIZES)
    log_a = jax.nn.log_sigmoid((glr @ gate_w + gate_b).astype(jnp.float32)) / GLA_TAU
    hd = lambda t, n, d: t.reshape(B_, S, n, d)
    yc = gla(hd(gq, GLA_HEADS, GLA_DK), hd(gk, GLA_HEADS, GLA_DK), hd(gv, GLA_HEADS, GLA_DV),
             hd(log_a, GLA_HEADS, GLA_DK))
    yc = rmsnorm(yc, gla_norm_g).reshape(B_, S, GLA_VW)
    yd = stick_breaking(hd(sq, SB_HEADS, SB_HEAD_DIM), hd(sk, SB_HEADS, SB_HEAD_DIM),
                        hd(sv, SB_HEADS, SB_HEAD_DIM)).reshape(B_, S, SB_WIDTH)
    y = jnp.concatenate([yc, yd], axis=-1) * jax.nn.silu(gate)
    return x + gate_res * (y @ out_w)

def second_inputs(seed: int = 0) -> dict:
    key = jax.random.key(seed)
    ks = jax.random.split(key, 20)
    nrm = lambda k, shape, s: jax.random.normal(k, shape, jnp.float32) * s
    return {
        "x": nrm(ks[0], (BATCH, SEQ, D_MODEL), 1.0),
        "c": nrm(ks[1], (BATCH, D_MODEL), 1.0),
        "ada_w": nrm(ks[2], (DEPTH_2, D_MODEL, 3 * D_MODEL), 0.5 * D_MODEL ** -0.5),
        "ada_b": nrm(ks[3], (DEPTH_2, 3 * D_MODEL), 0.02),
        "norm_g": 1.0 + nrm(ks[4], (DEPTH_2, D_MODEL), 0.05),
        "even_in_w": nrm(ks[5], (N_EVEN, D_MODEL, EVEN_IN), D_MODEL ** -0.5),
        "pool_w": nrm(ks[6], (N_EVEN, 4, POOL_GROUP, POOL_GROUP), POOL_GROUP ** -0.5),
        "pool_scale": 1.0 + nrm(ks[7], (N_EVEN, POOL_WIDTH), 0.1),
        "sgu_norm_g": 1.0 + nrm(ks[8], (N_EVEN, SGU_WIDTH), 0.05),
        "sgu_w": nrm(ks[9], (N_EVEN, SGU_HEADS, SGU_LEN, SGU_LEN), SGU_LEN ** -0.5),
        "sgu_b": 1.0 + nrm(ks[10], (N_EVEN, SGU_HEADS, SGU_LEN), 0.1),
        "even_out_w": nrm(ks[11], (N_EVEN, EVEN_MIX, D_MODEL), EVEN_MIX ** -0.5),
        "odd_in_w": nrm(ks[12], (N_ODD, D_MODEL, ODD_IN), D_MODEL ** -0.5),
        "gla_gate_w": nrm(ks[13], (N_ODD, GLA_RANK, GLA_KW), GLA_RANK ** -0.5),
        "gla_gate_b": nrm(ks[14], (N_ODD, GLA_KW), 0.1),
        "gla_norm_g": 1.0 + nrm(ks[15], (N_ODD, GLA_HEADS, GLA_DV), 0.05),
        "odd_out_w": nrm(ks[16], (N_ODD, ODD_MIX, D_MODEL), ODD_MIX ** -0.5),
        "final_g": 1.0 + nrm(ks[17], (D_MODEL,), 0.05),
    }

def second_block(x, c, ada_w, ada_b, norm_g, even_in_w, pool_w, pool_scale, sgu_norm_g, sgu_w, sgu_b,
              even_out_w, odd_in_w, gla_gate_w, gla_gate_b, gla_norm_g, odd_out_w, final_g):
    for i in range(DEPTH_2):
        j = i // 2
        if i % 2 == 0:
            x = even_layer(x, c, norm_g[i], ada_w[i], ada_b[i], even_in_w[j], pool_w[j], pool_scale[j],
                           sgu_norm_g[j], sgu_w[j], sgu_b[j], even_out_w[j])
        else:
            x = odd_layer(x, c, norm_g[i], ada_w[i], ada_b[i], odd_in_w[j], gla_gate_w[j], gla_gate_b[j],
                          gla_norm_g[j], odd_out_w[j])
    return rmsnorm(x, final_g)


def setup_inputs(seed=0):
    out = dict(first_inputs(seed))
    for name, value in second_inputs(seed + 1).items():
        if name != "x":
            out[name + "_2"] = value
    return out


def reference(
    x, meta_tokens, w_in, w_na_out, w_hg_out, w_o, w_up, w_down, norm_mix, norm_mlp, norm_final,
    hg_norm, na_rpb, hg_lb_logits, c_2, ada_w_2, ada_b_2, norm_g_2, even_in_w_2, pool_w_2,
    pool_scale_2, sgu_norm_g_2, sgu_w_2, sgu_b_2, even_out_w_2, odd_in_w_2, gla_gate_w_2,
    gla_gate_b_2, gla_norm_g_2, odd_out_w_2, final_g_2,
):
    x = first_block(
        x, meta_tokens, w_in, w_na_out, w_hg_out, w_o, w_up, w_down, norm_mix, norm_mlp,
        norm_final, hg_norm, na_rpb, hg_lb_logits,
    )
    return second_block(
        x, c_2, ada_w_2, ada_b_2, norm_g_2, even_in_w_2, pool_w_2, pool_scale_2, sgu_norm_g_2,
        sgu_w_2, sgu_b_2, even_out_w_2, odd_in_w_2, gla_gate_w_2, gla_gate_b_2, gla_norm_g_2,
        odd_out_w_2, final_g_2,
    )


_drawn_inputs = setup_inputs


def setup_inputs(seed=0):
    import zlib

    import numpy as np

    out = dict(_drawn_inputs(seed))
    spreads = {}
    factors = {'hg_norm': 3.026,
     'na_rpb': 6.484,
     'hg_lb_logits': 3.232,
     'pool_scale_2': 4.539,
     'sgu_norm_g_2': 8.0,
     'sgu_b_2': 3.517,
     'gla_gate_b_2': 7.006,
     'gla_norm_g_2': 8.0}
    for name, (base, spread) in spreads.items():
        noise = np.random.default_rng([zlib.crc32(name.encode()), seed]).standard_normal(out[name].shape)
        drawn = base * np.exp(spread * noise) if base else spread * noise
        out[name] = __import__('jax').numpy.asarray(drawn.astype(out[name].dtype))
    for name, factor in factors.items():
        out[name] = (out[name] * factor).astype(out[name].dtype)
    return out
```

```python
from contextlib import ExitStack

import numpy as np

import concourse.bass as bass
from concourse import mybir

F32 = mybir.dt.float32
F32R = mybir.dt.float32r
U8 = mybir.dt.uint8
ALU = mybir.AluOpType
ACT = mybir.ActivationFunctionType
AX = mybir.AxisListType

EPS = 1e-6
NRAW = 6
NSPLIT = 5
AHEAD = 3
LN_SET = "natural_log_exp_and_others"
EXP_SET = "exp_and_others"

PCOLS = {}
for _n, _w in [("norm_mix", 8), ("norm_mlp", 8), ("norm_final", 8), ("hg_norm", 4), ("lb", 16), ("c", 8),
               ("ada_b", 48), ("norm_g", 16), ("pool_scale", 8), ("sgu_g", 8), ("gate_b", 4), ("gla_g", 8),
               ("final_g", 8)]:
    PCOLS[_n] = (sum(w for _, w in PCOLS.values()), _w)
NPAR = sum(w for _, w in PCOLS.values())

CCOLS = {}
for _n, _w in [("ident", 128), ("ones", 128), ("negones", 128), ("neguc", 128), ("strict", 128), ("negsb", 128),
               ("m64", 64), ("negwin", 64), ("cinv", 64), ("tril", 128)]:
    CCOLS[_n] = (sum(w for _, w in CCOLS.values()), _w)
NCST = sum(w for _, w in CCOLS.values())


def plan():
    out = []

    def mat(name, c0, c1, k0=0, nk=8, w=256):
        for c in range(c0, c1, w):
            for k in range(k0, k0 + nk, 4):
                out.append(("m", name, k, 4, c, w))

    mat("w_in", 512, 1024)
    mat("w_in", 0, 512)
    mat("w_in", 1024, 1536)
    mat("w_in", 2048, 2560)
    mat("w_in", 2560, 3072)
    mat("w_in", 1536, 2048)
    mat("w_in", 3072, 3584)
    mat("w_in", 3584, 6144)
    mat("w_na_out", 0, 1024, nk=4)
    mat("w_hg_out", 0, 1024, nk=4)
    mat("w_o", 0, 1024)
    mat("w_up", 0, 256)
    for g in range(4):
        mat("w_up", 1024 * g + 256, 1024 * g + 1024)
        if g < 3:
            mat("w_up", 1024 * g + 1024, 1024 * g + 1280)
        mat("w_down", 0, 1024, k0=8 * g)
    first = len(out)
    mat("even_in", 0, 1024)
    mat("even_in", 3072, 4096)
    mat("even_in", 2048, 3072)
    out.append(("m", "pool_w", 0, 4, 0, 256))
    out.append(("m", "pool_w", 4, 4, 0, 256))
    mat("even_in", 1024, 2048)
    mat("even_in", 4096, 5120)
    mat("even_out", 0, 1024)
    mat("even_out", 0, 1024, k0=8)
    mat("odd_in", 0, 1024)
    out.append(("m", "odd_in", 0, 8, 2048, 128))
    mat("odd_in", 1024, 2048)
    mat("odd_in", 5136, 7184)
    for p in range(4):
        mat("odd_in", 2064 + 256 * p, 2320 + 256 * p)
        mat("odd_in", 3088 + 256 * p, 3344 + 256 * p)
        mat("odd_in", 4112 + 256 * p, 4368 + 256 * p)
    mat("odd_out", 0, 1024)
    mat("odd_out", 0, 1024, k0=8)
    ada = [("a", i, g, k) for i in range(2) for g in range(6) for k in range(0, 8, 2)]
    res = []
    for n, u in enumerate(out):
        res.append(u)
        if 8 <= n < first and n % 2 == 1 and ada:
            res.append(ada.pop(0))
    assert not ada
    return res


GEN = type(x for x in ())


def lockstep(runs):
    res = [None if type(r) is GEN else r for r in runs]
    live = [n for n, r in enumerate(runs) if type(r) is GEN]
    while live:
        for n in list(live):
            try:
                next(runs[n])
            except StopIteration as e:
                res[n] = e.value
                live.remove(n)
    return res


def in_turn(*runs):
    runs = list(runs)
    while runs:
        for r in list(runs):
            try:
                next(r)
            except StopIteration:
                runs.remove(r)
                continue
            yield


def bc(ap, dims):
    return bass.AP(ap.tensor, ap.offset, [list(ap.ap[0])] + [list(d) for d in dims])


def activation_(*a, **k):
    return lambda e: e.activation(*a, **k)


def copy_(*a, **k):
    return lambda e: e.copy(*a, **k)


def copy_predicated_(*a, **k):
    return lambda e: e.copy_predicated(*a, **k)


def dma_start_(*a, **k):
    return lambda e: e.dma_start(*a, **k)


def matmul_(*a, **k):
    return lambda e: e.matmul(*a, **k)


def memset_(*a, **k):
    return lambda e: e.memset(*a, **k)


def mul_(*a, **k):
    return lambda e: e.mul(*a, **k)


def preload_act_table_set_(*a, **k):
    return lambda e: e.preload_act_table_set(*a, **k)


def reciprocal_(*a, **k):
    return lambda e: e.reciprocal(*a, **k)


def scalar_tensor_tensor_(*a, **k):
    return lambda e: e.scalar_tensor_tensor(*a, **k)


def tensor_copy_(*a, **k):
    return lambda e: e.tensor_copy(*a, **k)


def tensor_reduce_(*a, **k):
    return lambda e: e.tensor_reduce(*a, **k)


def tensor_scalar_(*a, **k):
    return lambda e: e.tensor_scalar(*a, **k)


def tensor_tensor_(*a, **k):
    return lambda e: e.tensor_tensor(*a, **k)


def tensor_tensor_scan_(*a, **k):
    return lambda e: e.tensor_tensor_scan(*a, **k)


def transpose_(*a, **k):
    return lambda e: e.transpose(*a, **k)


class Queue:

    def __init__(self, name, sem):
        self.name, self.sem, self.n, self.items, self.seen = name, sem, 0, [], {}

    def wait(self, tokens):
        need = {}
        for t in tokens:
            if t is None:
                continue
            if isinstance(t, list):
                for s, v in t:
                    need[s] = max(need.get(s, 0), v)
            else:
                need[t[0]] = max(need.get(t[0], 0), t[1])
        for s, v in need.items():
            if self.seen.get(s, 0) < v:
                self.seen[s] = v
                self.items.append(("w", s, v))

    def do(self, fn, *after, inc=True):
        self.wait(after)
        self.items.append(("i", fn, inc))
        if inc is True:
            self.n += 1
        return (self.sem, self.n)

    def emit(self, eng):
        for it in self.items:
            if it[0] == "w":
                eng.wait_ge(it[1], it[2])
            else:
                ins = it[1](eng)
                if it[2] is True:
                    ins.then_inc(self.sem, 1)
                elif it[2]:
                    ins.then_inc(it[2], 16)


class Ring:

    def __init__(self, bufs):
        self.bufs, self.free, self.i = bufs, [None] * len(bufs), 0

    def take(self):
        for _ in self.bufs:
            n = self.i % len(self.bufs)
            self.i += 1
            if self.free[n] != "taken":
                break
        tok = self.free[n]
        assert tok != "taken"
        self.free[n] = "taken"
        return n, self.bufs[n], tok

    def give(self, n, tokens):
        self.free[n] = tokens


def build(nc, ws, par, cst, msk, xt, biasd, gwd, bsd, wtd, out):
    items = plan()
    ctx = ExitStack()
    with ctx:
        def sbt(stack, name, shape, dt=F32):
            return stack.enter_context(nc.sbuf_tensor(name, shape, dt))

        def sem(name):
            return ctx.enter_context(nc.semaphore(name))

        pe, act, dve, pool, sp = (Queue(n, sem("s_" + n)) for n in ("pe", "act", "dve", "pool", "sp"))

        raw = sbt(ctx, "raw", [128, NRAW, 1024])
        wh = sbt(ctx, "wh", [128, NSPLIT, 1024], F32R)
        wl = sbt(ctx, "wl", [128, NSPLIT, 1024], F32R)
        XAh = sbt(ctx, "XAh", [128, 8, 272], F32R)
        XAl = sbt(ctx, "XAl", [128, 8, 272], F32R)
        B0h = sbt(ctx, "B0h", [128, 8, 256], F32R)
        B0l = sbt(ctx, "B0l", [128, 8, 256], F32R)
        h = sbt(ctx, "h", [128, 8, 272])
        P = sbt(ctx, "P", [128, NPAR])
        C = sbt(ctx, "C", [128, NCST])
        K8 = sbt(ctx, "K8", [128, 7, 128], U8)
        rsB = sbt(ctx, "rsB", [128, 272])
        lnb = sbt(ctx, "lnb", [128, 272])
        sq = Ring([sbt(ctx, f"sq{i}", [128, 272]) for i in range(4)])
        vt = Ring([sbt(ctx, f"vt{i}", [128, 272]) for i in range(3)])
        th = Ring([sbt(ctx, f"th{i}", [128, 272]) for i in range(2)])
        adaT = sbt(ctx, "adaT", [128, 2, 24])
        G1 = sbt(ctx, "G1", [128, 2, 8])
        hp = sbt(ctx, "hp", [128, 28])
        lbw = sbt(ctx, "lbw", [128, 6, 8])
        cs = sbt(ctx, "cs", [128, 2, 8])
        accs = [sbt(ctx, f"acc{i}", [128, 512]) for i in range(2)]

        banks = [ctx.enter_context(nc.psum_tensor(f"bank{i}", [128, 512], F32)) for i in range(8)]
        main, sideb = Ring(banks[:4]), Ring(banks[4:])

        def par_(name, i=0):
            a = PCOLS[name][0]
            return P[:, a + i:a + i + 1]

        def pars(name, i=0, n=None):
            a, w = PCOLS[name]
            return P[:, a + i:a + i + (n or w)]

        def cst_(name, n=None):
            a, w = CCOLS[name]
            return C[:, a:a + (n or w)]

        def load(name, dst, src, *after, q=sp):
            s = sem("l_" + name)
            q.do(dma_start_(dst, src), *after, inc=s)
            return (s, 16)

        t_x = load("x", h[:, :, :], xt)
        t_par = load("par", P[:, :], par, q=act)
        t_cst = load("cst", C[:, :], cst, q=act)

        raw_sem = [sem(f"raw{i}") for i in range(NRAW)]
        used = [None] * len(items)
        loaded = [0]
        fed = [0]
        mains = [None]
        splits = []
        split_ring = [None] * NSPLIT
        unit_no = [0]

        def load_until(n):
            while loaded[0] < min(n, len(items)):
                i = loaded[0]
                r = raw[:, i % NRAW, :]
                sp.do(dma_start_(r, ws[i]), used[i - NRAW] if i >= NRAW else None,
                      inc=raw_sem[i % NRAW])
                loaded[0] += 1

        acc_free = [None, None]
        ada_state = {"n": 0, "tok": None}
        ada_jobs = []

        def feed():
            i = fed[0]
            it = items[i]
            load_until(i + NRAW)
            slot = raw[:, i % NRAW, :]
            landed = (raw_sem[i % NRAW], 16 * (i // NRAW + 1))
            if it[0] == "m":
                j = len(splits)
                hi, lo = wh[:, j % NSPLIT, :], wl[:, j % NSPLIT, :]
                a = act.do(copy_(hi, slot), landed, split_ring[j % NSPLIT])
                b = dve.do(tensor_tensor_(lo, slot, hi.bitcast(F32), ALU.subtract), landed, a,
                           split_ring[j % NSPLIT])
                splits.append([a, b])
                used[i] = [b]
            else:
                _, layer, g, k = it
                cyc = g % 2
                acc = accs[cyc]
                for kk in (k, k + 1):
                    col = cs[:, 1, kk:kk + 1]
                    part = raw[:, i % NRAW, 512 * (kk - k):512 * (kk - k) + 512]
                    if kk == 0:
                        t = dve.do(tensor_scalar_(acc[:, :], part, col, None, ALU.mult), landed, t_cs,
                                   acc_free[cyc])
                    else:
                        t = dve.do(scalar_tensor_tensor_(acc[:, :], part, col, acc[:, :], ALU.mult,
                                                                    ALU.add), landed, ada_state["tok"])
                    ada_state["tok"] = t
                used[i] = [t]
                if k == 6:
                    ada_jobs.append((layer, g, cyc, t))
            fed[0] += 1
            load_until(min(fed[0] + NRAW, len(items)))

        t_ada = {}

        def run_ada_jobs():
            while ada_jobs:
                layer, g, cyc, t = ada_jobs.pop(0)
                acc = accs[cyc]
                n, bk, fr = sideb.take()
                for c in range(4):
                    m = pe.do(matmul_(bk[:, 2 * c:2 * c + 1], acc[:, c * 128:c * 128 + 128],
                                                 cst_("ones", 1), start=True, stop=True), t, fr, t_cst,
                              inc=(c == 3))
                acc_free[cyc] = [m]
                d = dve.do(tensor_tensor_(adaT[:, layer, 4 * g:4 * g + 4], bk[:, 0:8:2],
                                                     pars("ada_b", 24 * layer + 4 * g, 4), ALU.add), m, t_par)
                sideb.give(n, [d])
                t_ada[(layer, g)] = d
                if g == 3:
                    t_ada[(layer, "G")] = dve.do(
                        scalar_tensor_tensor_(G1[:, layer, :], adaT[:, layer, 8:16], 1.0,
                                                         pars("norm_g", 8 * layer, 8), ALU.add, ALU.mult), d,
                        t_ada[(layer, 2)])

        side = []

        def step(n=1):
            for _ in range(n):
                while side:
                    try:
                        next(side[0])
                        break
                    except StopIteration:
                        side.pop(0)

        def drain():
            while side:
                step()

        steps = {"n": 1}
        after_pe = []

        def unit(spec):
            j = unit_no[0]
            while len(splits) < j + 1 + AHEAD and fed[0] < len(items):
                feed()
            it = [x for x in items_m[j]]
            assert tuple(it[1:]) == tuple(spec), (it, spec)
            unit_no[0] += 1
            w = it[5]
            v = "p (k n) -> p k n"
            return (j, wh[:, j % NSPLIT, :].rearrange(v, n=w), wl[:, j % NSPLIT, :].rearrange(v, n=w), splits[j])

        items_m = [x for x in items if x[0] == "m"]

        def unit_done(j, tok):
            split_ring[j % NSPLIT] = [tok]

        def three(dst, a, b, first, last, wait, fin, wfirst):
            order = [(1, 0), (0, 0), (0, 1)] if wfirst else [(0, 1), (0, 0), (1, 0)]
            for n, (i, j) in enumerate(order):
                t = pe.do(matmul_(dst, a[i], b[j], start=first and n == 0,
                                                           stop=last and n == 2), *wait,
                          inc=(fin and n == 2))
            return t

        def run_t(name, c0, c1, X, xt_, evac, k0=0, nk=8, n0=0, n1=272, w=256, xk=0, t0=0):
            tile = t0
            for c in range(c0, c1, w):
                nb = w // 128
                bs = [main.take() for _ in range(nb)]
                quads = range(0, nk, 8 if w == 128 else 4)
                for q in quads:
                    kn = 8 if w == 128 else 4
                    j, hi, lo, stk = unit((name, k0 + q, kn, c, w))
                    for k in range(kn):
                        for b in range(nb):
                            last = q + k == nk - 1
                            s = slice(b * 128, b * 128 + 128)
                            m = three(bs[b][1][:, 0:n1 - n0], (hi[:, k, s], lo[:, k, s]),
                                      (X[0][:, xk + q + k, n0:n1], X[1][:, xk + q + k, n0:n1]),
                                      q + k == 0, last, (stk, bs[b][2], xt_[xk + q + k]),
                                      last or (k == kn - 1 and b == nb - 1), True)
                            if last:
                                bs[b] += (m,)
                    unit_done(j, m)
                    if q + 4 < nk and w == 256:
                        step(steps["n"])
                for f in after_pe:
                    f()
                run_ada_jobs()
                step(steps["n"])
                for b, r in enumerate(lockstep([evac(tile + b, bs[b][1], bs[b][3]) for b in range(nb)])):
                    main.give(bs[b][0], r)
                tile += nb

        def run_n(name, c0, c1, X, xt_, tiles, evac):
            for c in range(c0, c1, 256):
                bs = [main.take() for _ in tiles]
                for q in (0, 4):
                    j, hi, lo, stk = unit((name, q, 4, c, 256))
                    for b, t0 in enumerate(tiles):
                        for k in range(4):
                            last = q + k == 7
                            m = three(bs[b][1][:, 0:256], (X[0][:, q + k, t0:t0 + 128], X[1][:, q + k, t0:t0 + 128]),
                                      (hi[:, k, :], lo[:, k, :]), q + k == 0, last,
                                      (stk, bs[b][2], xt_[q + k]), last or (k == 3 and b == len(tiles) - 1), False)
                            if last:
                                bs[b] += (m,)
                    unit_done(j, m)
                    if q == 0:
                        step(steps["n"])
                run_ada_jobs()
                step(steps["n"])
                for b, r in enumerate(lockstep([evac(b, c - c0, bs[b][1], bs[b][3]) for b in range(len(tiles))])):
                    main.give(bs[b][0], r)

        def barrier():
            now = [(q.sem, q.n) for q in (pe, act, dve, pool)]
            for q in (act, dve, pool):
                q.wait(now)

        def hilo_g(dst, v, *after):
            a = act.do(copy_(dst[0], v), *after)
            yield
            return [a, dve.do(tensor_tensor_(dst[1], v, dst[0].bitcast(F32), ALU.subtract), a, *after)]

        def hilo(dst, v, *after):
            return lockstep([hilo_g(dst, v, *after)])[0]

        def feed_ahead():
            while len(splits) < unit_no[0] + NSPLIT - 1 and fed[0] < len(items):
                feed()

        def rsqrt(dst, src, tmp, scale, *after):
            a = act.do(activation_(tmp, src, ACT.Ln, bias=EPS, scale=scale), *after)
            return act.do(activation_(dst, tmp, ACT.Exp, scale=-0.5), a)

        class Stats:

            def __init__(self, X, N, off=0, scale=None):
                self.scale = scale
                self.X, self.N, self.off, self.todo, self.n = X, N, off, [], 0
                self.bank = None

            def square(self, k, tok):
                i, s, f = sq.take()
                a = act.do(activation_(s[:, 0:self.N], self.X[:, k, self.off:self.off + self.N], ACT.Square,
                                       scale=1.0 if self.scale is None else self.scale(k)), tok, f)
                self.todo.append((i, s, a))

            def sums(self):
                if self.bank is None:
                    self.bank = sideb.take()
                _, bk, fr = self.bank
                while self.todo:
                    i, s, a = self.todo.pop(0)
                    self.m = pe.do(matmul_(bk[:, 0:self.N], cst_("ones"), s[:, 0:self.N], start=self.n == 0,
                                           stop=self.n == 7), a, fr, t_cst)
                    sq.give(i, [self.m])
                    self.n += 1

            def finish(self):
                self.sums()
                assert self.n == 8
                n, bk, _ = self.bank
                act.do(preload_act_table_set_(LN_SET), inc=False)
                t = rsqrt(rsB[:, 0:self.N], bk[:, 0:self.N], lnb[:, 0:self.N], 1.0 / 1024, self.m, rs_readers[0])
                act.do(preload_act_table_set_(EXP_SET), inc=False)
                sideb.give(n, [t])
                return t

        def stats(X, toks, N, off=0):
            s = Stats(X, N, off)
            for k in range(8):
                s.square(k, toks[k])
                s.sums()
            return s.finish()

        rs_readers = [None]

        def apply(X, toks, N, off, trs, gcol, scol, dst, dtok, rs=rsB):
            res = []
            late = []

            def low():
                k, i, v, a, b = late.pop(0)
                c = dve.do(tensor_tensor_(dst[1][:, k, 0:N], v[:, 0:N], dst[0][:, k, 0:N].bitcast(F32), ALU.subtract),
                           b, dtok)
                vt.give(i, [b, c])
                res.append([b, c])

            for k in range(8):
                i, v, f = vt.take()
                if scol is None:
                    a = dve.do(scalar_tensor_tensor_(v[:, 0:N], X[:, k, off:off + N], gcol(k), rs[:, 0:N], ALU.mult,
                                                     ALU.mult), trs, toks[k], f, t_par)
                    rs_readers[0] = [a]
                else:
                    i2, u, f2 = th.take()
                    b = dve.do(tensor_tensor_(u[:, 0:N], X[:, k, off:off + N], rs[:, 0:N], ALU.mult), trs, toks[k],
                               f2)
                    if len(late) > 1:
                        low()
                    a = dve.do(tensor_scalar_(v[:, 0:N], u[:, 0:N], gcol(k), scol(k), ALU.mult, ALU.add), b, f, dtok)
                    th.give(i2, [a])
                    rs_readers[0] = [b]
                b = act.do(copy_(dst[0][:, k, 0:N], v[:, 0:N]), a, dtok)
                late.append((k, i, v, a, b))
                if len(late) > 1:
                    low()
            while late:
                low()
            return res

        t_hp = [dve.do(tensor_scalar_(hp[:, 0:4], pars("hg_norm"), 0.5, None, ALU.mult), t_par),
                dve.do(tensor_scalar_(hp[:, 4:12], pars("pool_scale"), 0.5, None, ALU.mult)),
                dve.do(tensor_scalar_(hp[:, 12:20], pars("gla_g"), 0.5, None, ALU.mult))]
        a = act.do(activation_(cs[:, 0, :], pars("c"), ACT.Tanh, scale=0.5), t_par)
        a = dve.do(scalar_tensor_tensor_(cs[:, 0, :], cs[:, 0, :], 1.0, pars("c"), ALU.add, ALU.mult), a)
        t_cs = dve.do(tensor_scalar_(cs[:, 1, :], cs[:, 0, :], 0.5, None, ALU.mult), a)
        lb4 = pars("lb").rearrange("p (d l h) -> p d l h", d=2, l=2)
        LB = [lbw[:, i, :].rearrange("p (d h) -> p d h", d=2) for i in range(6)]
        a = dve.do(tensor_tensor_(LB[0], lb4[:, :, 0, :], lb4[:, :, 1, :], ALU.max), t_par)
        b = dve.do(tensor_tensor_(LB[1], lb4[:, :, 0, :], LB[0], ALU.subtract), a)
        c_ = dve.do(tensor_tensor_(LB[2], lb4[:, :, 1, :], LB[0], ALU.subtract), a)
        b = act.do(activation_(LB[1], LB[1], ACT.Exp), b)
        c_ = act.do(activation_(LB[2], LB[2], ACT.Exp), c_)
        a = dve.do(tensor_tensor_(LB[0], LB[1], LB[2], ALU.add), b, c_)
        a = dve.do(reciprocal_(LB[3], LB[0]), a)
        b = dve.do(tensor_tensor_(LB[1], LB[1], LB[3], ALU.mult), a)
        c_ = dve.do(tensor_tensor_(LB[2], LB[2], LB[3], ALU.mult), a)
        a = dve.do(tensor_scalar_(LB[4], LB[2], 0.25, None, ALU.mult), c_)
        b = dve.do(scalar_tensor_tensor_(LB[0], LB[2], 0.5, LB[1], ALU.mult, ALU.add), b, c_)
        c_ = dve.do(tensor_scalar_(LB[3], LB[2], 0.5, None, ALU.mult), c_, b)
        t_lb = [a, b, c_, dve.do(tensor_scalar_(LB[5], LB[4], -1.0, None, ALU.mult), a)]

        def lbc(which, d, hh):
            i = {"fa": 0, "fb": 3, "kc": 4, "nkc": 5}[which]
            return lbw[:, i, 4 * d + hh:4 * d + hh + 1]

        def silu2(dst, ps, tok, *after):
            n = ps.shape[1]
            i, tt, f = th.take()
            a = act.do(activation_(tt[:, 0:n], ps, ACT.Tanh, scale=0.5), tok, f)
            yield
            b = dve.do(scalar_tensor_tensor_(dst, tt[:, 0:n], 1.0, ps, ALU.add, ALU.mult), a, *after)
            th.give(i, [b])
            return b

        ph1 = ExitStack()
        ff = sbt(ph1, "ff", [128, 4, 256])
        kf = sbt(ph1, "kf", [128, 4, 256])
        fb = sbt(ph1, "fb", [128, 4, 256])
        kb = sbt(ph1, "kb", [128, 4, 256])
        fm = sbt(ph1, "fm", [128, 2, 4, 16])
        q_ = sbt(ph1, "q_", [128, 4, 256])
        iN = sbt(ph1, "iN", [128, 2, 512])
        iM = sbt(ph1, "iM", [16, 512])
        gna = sbt(ph1, "gna", [128, 8, 256])
        pna = ExitStack()
        bias = sbt(pna, "bias", [128, 8, 384])
        qT = sbt(pna, "qT", [128, 4, 256])
        kT = sbt(pna, "kT", [128, 4, 272])
        vN = sbt(pna, "vN", [128, 2, 512])
        vM = sbt(pna, "vM", [16, 512])
        sP = Ring([sbt(pna, f"sP{i}", [128, 272]) for i in range(4)])
        PT = Ring([sbt(pna, f"PT{i}", [128, 2, 256]) for i in range(2)])
        PTm = [sbt(pna, f"PTm{i}", [16, 256]) for i in range(2)]
        nmr = Ring([sbt(pna, f"nm{i}", [128, 3]) for i in range(4)])

        t_bias = load("bias", bias[:, :, :], biasd, q=act)
        t_bias = pool.do(tensor_tensor_(
            bias[:, :, :].rearrange("p h (e w) -> p (h e) w", w=64),
            bias[:, :, :].rearrange("p h (e w) -> p (h e) w", w=64),
            bc(cst_("negwin"), [[0, 48], [1, 64]]), ALU.add), t_bias, t_cst)

        X = (XAh, XAl)
        feed_ahead()
        trs = stats(h, [t_x] * 8, 272)
        xt_ = apply(h, [t_x] * 8, 272, 0, trs, lambda k: par_("norm_mix", k), None, X, None)

        t_k, t_q, t_v, t_i, t_g = {}, {}, {}, {}, {}

        def ev_k(j, ps, tok):
            t_k[j] = act.do(copy_(kT[:, j, :], ps[:, 0:272]), tok)
            return [t_k[j]]

        def ev_q(j, ps, tok):
            t_q[j] = act.do(mul_(qT[:, j, :], ps[:, 0:256], 0.125), tok)
            return [t_q[j]]

        def ev_v(b, c, ps, tok):
            d, n = (vM[:, c:c + 256], 16) if b == 0 else (vN[:, b - 1, c:c + 256], 128)
            t = act.do(copy_(d, ps[0:n, 0:256]), tok)
            t_v.setdefault(c, []).append(t)
            return [t]

        run_t("w_in", 512, 1024, X, xt_, ev_k)
        run_t("w_in", 0, 512, X, xt_, ev_q, n0=16)
        run_n("w_in", 1024, 1536, X, xt_, (0, 16, 144), ev_v)

        def attention():
            prob, o_tok = {}, []
            for s in range(10):
                if s < 8:
                    hh = s
                    po = 64 * (hh % 2)
                    for t in range(2):
                        n, bk, fr = sideb.take()
                        m = pe.do(matmul_(
                            bk[:, 0:272], qT[po:po + 64, hh // 2, 128 * t:128 * t + 128],
                            kT[po:po + 64, hh // 2, :], start=True, stop=True), t_q[hh // 2], t_k[hh // 2], fr)
                        i, S, f = sP.take()
                        i2, nm, f2 = nmr.take()
                        a = dve.do(tensor_tensor_(
                            S[:, 16:272], bk[:, 16:272], bias[:, hh, 128 - 128 * t:384 - 128 * t], ALU.add),
                            m, f, t_bias)
                        b = dve.do(tensor_copy_(S[:, 0:16], bk[:, 0:16]), m)
                        sideb.give(n, [b])
                        a = dve.do(tensor_reduce_(nm[:, 0:1], S[:, :], AX.X, ALU.max,
                                                                         negate=True), a, b, f2)
                        a = act.do(activation_(S[:, :], S[:, :], ACT.Exp, bias=nm[:, 0:1],
                                                                      accum_out=nm[:, 1:2]), a)
                        prob[(hh, t)] = (i, S, i2, nm, a)
                        yield
                if 1 <= s <= 8:
                    hh = s - 1
                    ip, pt, f = PT.take()
                    ptm = PTm[ip]
                    cp = []
                    for t in range(2):
                        i, S, i2, nm, a = prob.pop((hh, t))
                        a = dve.do(reciprocal_(nm[:, 2:3], nm[:, 1:2]), a)
                        a = dve.do(tensor_scalar_(S[:, :], S[:, :], nm[:, 2:3], None,
                                                                         ALU.mult), a)
                        nmr.give(i2, [a])
                        n, bk, fr = sideb.take()
                        for r in range(2):
                            pe.do(transpose_(
                                bk[:, 128 * r:128 * r + 128], S[:, 16 + 128 * r:144 + 128 * r], cst_("ident")),
                                a, fr, t_cst, inc=False)
                        m = pe.do(transpose_(bk[0:16, 256:384], S[:, 0:16], cst_("ident")))
                        sP.give(i, [m])
                        b = act.do(copy_(
                            pt[:, :, 128 * t:128 * t + 128], bk[:, 0:256].rearrange("p (a c) -> p a c", a=2)), m, f)
                        c = act.do(copy_(
                            ptm[:, 128 * t:128 * t + 128], bk[0:16, 256:384]), m, f)
                        sideb.give(n, [c])
                        cp += [b, c]
                        yield
                    prob[hh] = (ip, pt, ptm, cp)
                if s >= 2:
                    hh = s - 2
                    po = 64 * (hh % 2)
                    ip, pt, ptm, cp = prob.pop(hh)
                    n, bk, fr = sideb.take()
                    o = bk[po:po + 64, 0:256]
                    tv = t_v[256 * (hh // 4)]
                    v_ = slice(64 * hh, 64 * hh + 64)
                    for r in range(2):
                        pe.do(matmul_(o, vN[:, r, v_], pt[:, r, :], start=r == 0,
                                                                        stop=False), cp, tv, fr, inc=False)
                    m = pe.do(matmul_(o, vM[:, v_], ptm[:, :], start=False,
                                                                     stop=True))
                    PT.give(ip, [m])
                    r_ = hilo((B0h[po:po + 64, hh // 2, :], B0l[po:po + 64, hh // 2, :]), o, m)
                    sideb.give(n, r_)
                    o_tok.append(r_)
                    yield
            t_ona[0] = [sum([o_tok[2 * j], o_tok[2 * j + 1]], []) for j in range(4)]

        t_ona = [None]
        side.append(attention())
        t_fb = {}

        def ev_z(d, f_, k_, par_d):
            def ev(j, ps, tok):
                N = 272 if d == 0 else 256
                o = N - 256
                i, tt, f = th.take()
                a = act.do(activation_(tt[:, 0:N], ps[:, 0:N], ACT.Tanh, scale=0.5), tok, f)
                yield
                r = [dve.do(tensor_scalar_(f_[:, j, :], tt[:, o:N], lbc("fb", d, j), lbc("fa", d, j),
                                                      ALU.mult, ALU.add), a, t_lb),
                     dve.do(tensor_scalar_(k_[:, j, :], tt[:, o:N], lbc("nkc", d, j), lbc("kc", d, j),
                                                      ALU.mult, ALU.add), a, t_lb)]
                if d == 0:
                    r += [dve.do(tensor_scalar_(fm[:, 0, j, :], tt[:, 0:16], lbc("fb", d, j),
                                                           lbc("fa", d, j), ALU.mult, ALU.add), a),
                          dve.do(tensor_scalar_(fm[:, 1, j, :], tt[:, 0:16], lbc("nkc", d, j),
                                                           lbc("kc", d, j), ALU.mult, ALU.add), a)]
                th.give(i, r)
                t_fb[(d, j)] = r
                return [a]
            return ev

        def ev_qh(j, ps, tok):
            t_g[("q", j)] = yield from silu2(q_[:, j, :], ps[:, 0:256], tok)
            return [t_g[("q", j)]]

        def ev_i(b, c, ps, tok):
            d, n = (iM[:, c:c + 256], 16) if b == 0 else (iN[:, b - 1, c:c + 256], 128)
            t = act.do(copy_(d, ps[0:n, 0:256]), tok)
            t_i.setdefault(c, []).append(t)
            return [t]

        steps["n"] = 2
        run_t("w_in", 2048, 2560, X, xt_, ev_z(0, ff, kf, 0))
        run_t("w_in", 2560, 3072, X, xt_, ev_z(1, fb, kb, 1), n0=16)
        run_t("w_in", 1536, 2048, X, xt_, ev_qh, n0=16)
        run_n("w_in", 3072, 3584, X, xt_, (0, 16, 144), ev_i)
        drain()
        pna.close()
        barrier()
        phg = ExitStack()
        SFs = [sbt(phg, f"SF{i}", [128, 2, 256]) for i in range(2)]
        EPs = [sbt(phg, f"EP{i}", [128, 2, 256]) for i in range(2)]
        SF, EP = SFs[0], EPs[0]
        XY = Ring([(sbt(phg, f"Xl{i}", [128, 2, 256]), sbt(phg, f"Yl{i}", [128, 2, 256])) for i in range(2)])
        AT = sbt(phg, "AT", [128, 4, 512])
        ATm = sbt(phg, "ATm", [16, 4, 256])
        Hm = sbt(phg, "Hm", [128, 4, 16])
        sg = sbt(phg, "sg", [128, 4, 256])
        oS = [XY.bufs[i // 2][0][:, i % 2, :] for i in range(4)]
        ghg = sbt(phg, "ghg", [128, 8, 256])

        m32 = AT[:, :, :].rearrange("p h c -> p (h c)")[:, 0:896]
        t_msk = load("msk", m32, msk, q=act)
        t_msk = dve.do(tensor_copy_(K8[:, :, :].rearrange("p l c -> p (l c)"), m32), t_msk)

        def halves(a, b):
            v = a.rearrange("p h (g two b) -> p (h g) two b", two=2, b=b)
            return v[:, :, 0, :], v[:, :, 1, :]

        def recurrence():
            t = pool.do(memset_(Hm[:, :, 15:16], 1.0))
            fmt = sum([t_fb[(0, j)] for j in range(4)], [])
            for s in range(14, -1, -1):
                t = pool.do(tensor_tensor_(Hm[:, :, s:s + 1], Hm[:, :, s + 1:s + 2],
                                                           fm[:, 0, :, s + 1:s + 2], ALU.mult), t, fmt)
            t_hm = pool.do(tensor_tensor_(Hm[:, :, :], Hm[:, :, :], fm[:, 1, :, :], ALU.mult), t)
            yield
            at_tok = {0: [], 1: []}
            upd_last = []

            def levels(g):
                SF, EP = SFs[g], EPs[g]
                hs = slice(2 * g, 2 * g + 2)
                F_, B_, KF, KB, Q = (z[:, hs, :] for z in (ff, fb, kf, kb, q_))
                dep = sum([t_fb[(d, j)] for d in range(2) for j in (2 * g, 2 * g + 1)], [])
                dep = dep + [t_g[("q", 2 * g)], t_g[("q", 2 * g + 1)]]
                init = [pool.do(memset_(SF[:, :, :], 1.0)), pool.do(memset_(EP[:, :, :], 1.0))]
                upd = init
                lev = -1
                cpy = None
                for b in (0, 1, 2, 4, 8, 16, 32, 64, 128, 256):
                    i, (Xl, Yl), f = XY.take()
                    if b == 0:
                        pr = [pool.do(tensor_tensor_(Xl[:, :, :], KF, KB, ALU.add), dep, f)]
                        y = Q
                    elif b < 256:
                        y = Yl[:, :, :]
                        fh, bh, kfh, kbh, qh, xh, yh, sh, eh = (halves(z, b) for z in (
                            F_, B_, KF, KB, Q, Xl[:, :, :], Yl[:, :, :], SF[:, :, :], EP[:, :, :]))
                        pr = [pool.do(tensor_tensor_(yh[1], qh[1], fh[1], ALU.mult), upd, f, dep),
                              pool.do(tensor_tensor_(yh[0], qh[0], bh[0], ALU.mult), upd),
                              pool.do(tensor_tensor_(xh[0], kfh[0], sh[0], ALU.mult), upd),
                              dve.do(tensor_tensor_(xh[1], kbh[1], eh[1], ALU.mult), upd, f, dep)]
                        u = [dve.do(tensor_tensor_(sh[0], sh[0], last_of(fh[1], b, b - 1), ALU.mult), pr, dep),
                             dve.do(tensor_tensor_(eh[1], eh[1], last_of(bh[0], b, 0), ALU.mult), pr)]
                        upd = [dve.do(tensor_tensor_(fh[1], fh[1], last_of(fh[0], b, b - 1), ALU.mult), u),
                               dve.do(tensor_tensor_(bh[0], bh[0], last_of(bh[1], b, 0), ALU.mult), u)] + u
                    else:
                        y = Yl[:, :, :]
                        pr = [pool.do(tensor_tensor_(Yl[:, :, :], Q, F_, ALU.mult), upd, f)]
                    yield
                    n, bk, fr = sideb.take()
                    if b <= 64:
                        for hh in range(2):
                            for t in range(2):
                                s = slice(128 * t, 128 * t + 128)
                                c0 = 256 * hh + 128 * t
                                m = pe.do(matmul_(bk[:, c0:c0 + 128], Xl[:, hh, s], y[:, hh, s],
                                                             start=True, stop=True), pr, fr,
                                          inc=(hh == 1 and t == 1))
                        src = bk[:, :].rearrange("p (h t c) -> p h t c", h=2, t=2)
                        dst = AT[:, hs, :].rearrange("p h (a c) -> p h a c", c=128)[:, :, 0::3, :]
                        if b == 0:
                            cpy = dve.do(tensor_copy_(dst, src), m, t_msk)
                        else:
                            mk = bc(K8[:, lev, :], [[0, 2], [0, 2], [1, 128]])
                            cpy = dve.do(copy_predicated_(dst, mk, src), m, cpy, t_msk)
                        lev += 1
                        sideb.give(n, [cpy])
                    elif b == 128:
                        for hh in range(2):
                            for t in range(2):
                                c0 = 256 * hh + 128 * t
                                so, to = (0, 128) if t == 0 else (128, 0)
                                m = pe.do(matmul_(bk[:, c0:c0 + 128], Xl[:, hh, so:so + 128],
                                                             y[:, hh, to:to + 128], start=True, stop=True), pr, fr,
                                          inc=(hh == 1 and t == 1))
                        src = bk[:, :].rearrange("p (h t c) -> p h t c", h=2, t=2)
                        dst = AT[:, hs, :].rearrange("p h (a c) -> p h a c", c=128)[:, :, 1:3, :]
                        c2 = act.do(copy_(dst, src), m)
                        sideb.give(n, [c2])
                        at_tok[g] += [cpy, c2]
                    else:
                        for hh in range(2):
                            m = pe.do(matmul_(bk[0:16, 256 * hh:256 * hh + 256], Hm[:, 2 * g + hh, :],
                                                         y[:, hh, :], start=True, stop=True), pr, t_hm, fr,
                                      inc=hh == 1)
                        c2 = act.do(copy_(ATm[:, hs, :],
                                                     bk[0:16, :].rearrange("p (h c) -> p h c", h=2)), m)
                        sideb.give(n, [c2])
                        at_tok[g] += [c2]
                        upd_last.extend(pr + upd)
                    XY.give(i, [m])

            yield from in_turn(levels(0), levels(1))
            oT = []
            sst = []
            ssb = []
            for hh in range(4):
                n, bk, fr = sideb.take()
                ti = t_i[256 * (hh // 2)]
                for t in range(2):
                    pe.do(matmul_(bk[:, 0:256], iN[:, t, 128 * hh:128 * hh + 128],
                                             AT[:, hh, 256 * t:256 * t + 256], start=t == 0, stop=False),
                          at_tok[hh // 2], ti, fr, inc=False)
                m = pe.do(matmul_(bk[:, 0:256], iM[:, 128 * hh:128 * hh + 128], ATm[:, hh, :],
                                             start=False, stop=True))
                d = dve.do(tensor_copy_(oS[hh], bk[:, 0:256]), m)
                sideb.give(n, [d])
                oT.append(d)
                yield
                i, s, f = sq.take()
                a = act.do(activation_(s[:, 0:256], oS[hh], ACT.Square), d, f)
                if hh % 2 == 0:
                    ssb.append(sideb.take())
                n, bk, fr = ssb[-1]
                m = pe.do(matmul_(bk[:, 256 * (hh % 2):256 * (hh % 2) + 256], cst_("ones"), s[:, 0:256],
                                             start=True, stop=True), a, fr)
                sq.give(i, [m])
                sst.append(m)
                yield
            act.do(preload_act_table_set_(LN_SET), inc=False)
            for r in range(2):
                n, bk, _ = ssb[r]
                v = (SF if r == 0 else EP)[:, :, :].rearrange("p h c -> p (h c)")
                t = rsqrt(v, bk[:, :], v, 1.0 / 128, sst[2 * r + 1], upd_last, XYdone(at_tok))
                sideb.give(n, [t])
                sst[r] = t
            act.do(preload_act_table_set_(EXP_SET), inc=False)
            yield
            t_ohg[0] = []
            for hh in range(4):
                rs = (SF if hh < 2 else EP)[:, hh % 2, :]
                a = dve.do(tensor_tensor_(oS[hh], oS[hh], rs, ALU.mult), oT[hh], sst[hh // 2],
                           sst_last(sst))
                a = dve.do(scalar_tensor_tensor_(oS[hh], oS[hh], hp[:, hh:hh + 1],
                                                            sg[:, hh, :], ALU.mult, ALU.mult), a, t_g[("g", hh)],
                           t_hp)
                t_ohg[0].append(hilo((B0h[:, 4 + hh, :], B0l[:, 4 + hh, :]), oS[hh], a))
                yield

        def XYdone(a):
            return a[0] + a[1]

        def sst_last(s):
            return list(s[0:4])

        def last_of(v, b, i):
            x = v[:, :, i:i + 1]
            return bass.AP(x.tensor, x.offset, [list(x.ap[0]), list(x.ap[1]), [0, b]])

        t_ohg = [None]

        def ev_g(j, ps, tok):
            t_g[("g", j)] = yield from silu2(sg[:, j, :], ps[:, 0:256], tok)
            return [t_g[("g", j)]]

        def ev_gate(dst, key):
            def ev(j, ps, tok):
                t_g[(key, j)] = act.do(activation_(dst[:, j, :], ps[:, 0:256], ACT.Tanh, scale=0.5), tok)
                return [t_g[(key, j)]]
            return ev

        def ev_g20(j, ps, tok):
            if j < 4:
                return ev_g(j, ps, tok)
            if j < 12:
                return ev_gate(gna, "na")(j - 4, ps, tok)
            return ev_gate(ghg, "hg")(j - 12, ps, tok)

        side.append(recurrence())
        steps["n"] = 1
        run_t("w_in", 3584, 6144, X, xt_, ev_g20, n0=16)

        t_mix = {}

        def ev_na(j, ps, tok):
            t_mix[j] = dve.do(scalar_tensor_tensor_(gna[:, j, :], gna[:, j, :], 1.0, ps[:, 0:256],
                                                               ALU.add, ALU.mult), tok, t_g[("na", j)])
            return [t_mix[j]]

        run_t("w_na_out", 0, 1024, (B0h, B0l), t_ona[0], ev_na, nk=4, n1=256)
        drain()
        t_x2 = {}
        xa_free = [(pe.sem, pe.n)]

        def ev_hg(j, ps, tok):
            a = dve.do(scalar_tensor_tensor_(ghg[:, j, :], ghg[:, j, :], 1.0, ps[:, 0:256], ALU.add,
                                                        ALU.mult), tok, t_g[("hg", j)])
            b = dve.do(tensor_tensor_(gna[:, j, :], gna[:, j, :], ghg[:, j, :], ALU.add), a, t_mix[j])
            yield
            t_x2[j] = yield from hilo_g((XAh[:, j, 0:256], XAl[:, j, 0:256]), gna[:, j, :], b, xa_free)
            return [a]

        run_t("w_hg_out", 0, 1024, (B0h, B0l), [None] * 4 + t_ohg[0], ev_hg, nk=4, n1=256, xk=4)
        t_h = {}

        def ev_o(j, ps, tok):
            t_h[j] = dve.do(scalar_tensor_tensor_(h[:, j, 16:272], ps[:, 0:256], 0.5, h[:, j, 16:272],
                                                             ALU.mult, ALU.add), tok)
            yield
            st.square(j, t_h[j])
            return [t_h[j]]

        def summed():
            s = Stats(h, 256, 16)
            after_pe.append(s.sums)
            return s

        st = summed()
        run_t("w_o", 0, 1024, X, t_x2, ev_o, n1=256)
        phg.close()
        ph1.close()

        barrier()
        ph2 = ExitStack()
        B1h = sbt(ph2, "B1h", [128, 8, 256], F32R)
        B1l = sbt(ph2, "B1l", [128, 8, 256], F32R)
        B = [(B0h, B0l), (B1h, B1l)]
        r12 = sbt(ph2, "r12", [128, 256])
        nfG = sbt(ph2, "nfG", [128, 8])
        u2 = Ring([sbt(ph2, f"u2{i}", [128, 256]) for i in range(3)])
        after_pe.clear()
        trs = st.finish()
        feed_ahead()
        xt_ = apply(h, [t_h[k] for k in range(8)], 256, 16, trs, lambda k: par_("norm_mlp", k), None, X,
                    [(pe.sem, pe.n)])
        b_free = [[(pe.sem, pe.n)], None]

        def ev_add(gate=None, st=None):
            def ev(j, ps, tok):
                sc = 1.0 if gate is None else gate(j)
                t_h[j] = dve.do(scalar_tensor_tensor_(h[:, j, 16:272], ps[:, 0:256], sc,
                                                                 h[:, j, 16:272], ALU.mult, ALU.add), tok)
                if st is not None:
                    yield
                    for x in st:
                        x.square(j, t_h[j])
                return [t_h[j]]
            return ev

        def up(g, t_u):
            def ev(j, ps, tok):
                i, r, f = th.take()
                a = act.do(activation_(r[:, 0:256], ps[:, 0:256], ACT.Relu), tok, f)
                i2, u, f2 = u2.take()
                yield
                b = dve.do(tensor_tensor_(u[:, :], r[:, 0:256], r[:, 0:256], ALU.mult), a, f2)
                th.give(i, [b])
                t_u[j] = yield from hilo_g((B[g % 2][0][:, j, :], B[g % 2][1][:, j, :]), u[:, :], b, b_free[g % 2])
                u2.give(i2, t_u[j])
                return [a]
            return ev

        t_us = [{} for g in range(4)]
        run_t("w_up", 0, 256, X, xt_, up(0, t_us[0]), n1=256)
        for g in range(4):
            run_t("w_up", 1024 * g + 256, 1024 * g + 1024, X, xt_, up(g, t_us[g]), n1=256, t0=2)
            if g < 3:
                run_t("w_up", 1024 * g + 1024, 1024 * g + 1280, X, xt_, up(g + 1, t_us[g + 1]), n1=256)
            else:
                st = summed()
                st2 = Stats(h, 256, 16, lambda k: par_("norm_final", k))
                after_pe.append(st2.sums)
            run_t("w_down", 0, 1024, B[g % 2], t_us[g], ev_add(st=[st, st2] if g == 3 else None), k0=8 * g, n1=256)
            b_free[g % 2] = [(pe.sem, pe.n)]

        H = [t_h[k] for k in range(8)]
        after_pe.clear()
        st2.sums()
        trs = st.finish()
        n, bk, _ = st2.bank
        a = dve.do(tensor_tensor_(r12[:, :], rsB[:, 0:256], rsB[:, 0:256], ALU.mult), trs)
        a = dve.do(tensor_tensor_(r12[:, :], bk[:, 0:256], r12[:, :], ALU.mult), a, st2.m)
        sideb.give(n, [a])
        a = rsqrt(r12[:, :], r12[:, :], lnb[:, 0:256], 1.0 / 1024, a)
        act.do(preload_act_table_set_(EXP_SET), inc=False)
        trs = dve.do(tensor_tensor_(r12[:, :], r12[:, :], rsB[:, 0:256], ALU.mult), a)
        feed_ahead()
        ph3 = ExitStack()
        barrier()
        aP = sbt(ph3, "aP", [128, 8, 272])
        s1 = sbt(ph3, "s1", [128, 2, 272])
        s2 = sbt(ph3, "s2", [128, 2, 272])
        pf = Ring([sbt(ph3, f"pf{i}", [128, 2, 256]) for i in range(2)])
        ga = sbt(ph3, "ga", [128, 8, 256])
        gb = sbt(ph3, "gb", [128, 8, 256])
        vn = sbt(ph3, "vn", [128, 2, 1024])
        ss = sbt(ph3, "ss", [128, 2, 8])
        wT = sbt(ph3, "wT", [128, 8, 128])
        bS = sbt(ph3, "bS", [128, 8, 128])
        mark = [(q.sem, q.n) for q in (act, dve, pool, pe)]
        t_wT = load("wT", wT[:, :, :], wtd, mark)
        t_bS = load("bS", bS[:, :, :], bsd, mark)
        t_wT = pool.do(tensor_tensor_(wT[:, :, :], wT[:, :, :],
                                                 bc(cst_("tril"), [[0, 8], [1, 128]]), ALU.mult), t_wT, t_cst)
        t_pad = [pool.do(memset_(aP[:, :, 0:16], 0.0)), pool.do(memset_(s1[:, :, 0:16], 0.0)),
                 pool.do(memset_(s2[:, :, 0:16], 0.0))]

        t_nfG = dve.do(tensor_tensor_(nfG[:, :], pars("norm_final"), G1[:, 0, :], ALU.mult), t_ada[(0, "G")], t_par)

        def ada_ready(layer):
            return [t_ada[(layer, g)] for g in range(6)] + [t_ada[(layer, "G")]]

        xt_ = apply(h, H, 256, 16, trs, lambda k: nfG[:, k:k + 1], lambda k: adaT[:, 0, k:k + 1], X,
                    [(pe.sem, pe.n), t_nfG] + ada_ready(0), r12)
        for k in range(8):
            t_h[k] = dve.do(scalar_tensor_tensor_(h[:, k, 16:272], h[:, k, 16:272], par_("norm_final", k),
                                                  rsB[:, 0:256], ALU.mult, ALU.mult), xt_[k], H[k])
        rs_readers[0] = [t_h[7]]

        t_a, t_ga, t_gb, t_vn, t_p = {}, {}, {}, {0: [], 1: []}, {}

        def ev_a(j, ps, tok):
            t_a[j] = act.do(copy_(aP[:, j, 16:272], ps[:, 0:256]), tok)
            return [t_a[j]]

        def ev_silu2(dst, toks):
            def ev(j, ps, tok):
                toks[j] = yield from silu2(dst[:, j, :], ps[:, 0:256], tok)
                return [toks[j]]
            return ev

        def ev_vn(b, c, ps, tok):
            t = act.do(copy_(vn[:, b, c:c + 256], ps[:, 0:256]), tok)
            t_vn[b].append(t)
            return [t]

        b1f = b_free[1]
        b0f = b_free[0]

        def pool_side():
            fin = {}
            for g in range(4):
                src = aP[:, 2 * g:2 * g + 2, :]
                t = [t_a[2 * g], t_a[2 * g + 1]] + t_pad
                last = fin.get(g - 1)
                cur, sh = src, 1
                for n in range(g + 1):
                    o = (s1, s2)[n % 2]
                    t = [pool.do(tensor_tensor_(o[:, :, 16:272], cur[:, :, 16:272],
                                                           cur[:, :, 16 - sh:272 - sh], ALU.add), t, last)]
                    cur, sh = o, 2 * sh
                i, p, f = pf.take()
                w = 2 << g
                a = dve.do(scalar_tensor_tensor_(p[:, :, :], cur[:, :, 16:272], 1.0 / w,
                                                            src[:, :, 16:272], ALU.mult, ALU.subtract), t, f)
                b = dve.do(tensor_tensor_(p[:, :, 0:16], cur[:, :, 16:32],
                                                     bc(cst_("cinv")[:, 16 * g:16 * g + 16], [[0, 2], [1, 16]]),
                                                     ALU.mult), a)
                a = dve.do(tensor_tensor_(p[:, :, 0:16], p[:, :, 0:16], src[:, :, 16:32],
                                                     ALU.subtract), b)
                fin[g] = [b]
                for j in range(2):
                    t_p[2 * g + j] = hilo((B1h[:, 2 * g + j, :], B1l[:, 2 * g + j, :]), p[:, j, :], a, b1f)
                pf.give(i, t_p[2 * g] + t_p[2 * g + 1])
                yield

        steps["n"] = 1
        run_t("even_in", 0, 1024, X, xt_, ev_a, n1=256)
        side.append(pool_side())
        run_t("even_in", 3072, 4096, X, xt_, ev_silu2(ga, t_ga), n1=256)
        run_n("even_in", 2048, 3072, X, xt_, (0, 128), ev_vn)
        drain()
        t_ya = {}
        for g in range(4):
            if g % 2 == 0:
                j, hi, lo, stk = unit(("pool_w", 2 * g, 4, 0, 256))
            bs = [main.take() for _ in range(2)]
            for b in range(2):
                for k in range(2):
                    s = slice(b * 128, b * 128 + 128)
                    kk = 2 * (g % 2) + k
                    m = three(bs[b][1][:, 0:256], (hi[:, kk, s], lo[:, kk, s]),
                              (B1h[:, 2 * g + k, :], B1l[:, 2 * g + k, :]), k == 0, k == 1,
                              (stk, bs[b][2], t_p[2 * g + k]), k == 1, True)
                jj = 2 * g + b
                i, v, f = vt.take()
                a = dve.do(scalar_tensor_tensor_(v[:, 0:256], bs[b][1][:, 0:256], hp[:, 4 + jj:5 + jj],
                                                            ga[:, jj, :], ALU.mult, ALU.mult), m, f, t_ga[jj])
                main.give(bs[b][0], [a])
                t_ya[jj] = hilo((B0h[:, jj, :], B0l[:, jj, :]), v[:, 0:256], a, b0f)
                vt.give(i, t_ya[jj])
            unit_done(j, m)
        b1_free2 = [(pe.sem, pe.n)]

        uT = aP
        t_u = {}

        def ev_u(j, ps, tok):
            t_u[j] = act.do(mul_(uT[:, j, 16:272], ps[:, 0:256], 0.5), tok, pool_done)
            return [t_u[j]]

        pool_done = [(pool.sem, pool.n), (dve.sem, dve.n)]
        t_yb = {}

        def ev_gb(j, ps, tok):
            a = yield from silu2(gb[:, j, :], ps[:, 0:256], tok)
            t_gb[j] = dve.do(tensor_tensor_(gb[:, j, :], gb[:, j, :], uT[:, j, 16:272], ALU.mult), a,
                             t_u[j])
            return [a]

        def sgu():
            rv = []
            for b in range(2):
                j, p, f = pf.take()
                w = p[:, :, :].rearrange("p a c -> p (a c)")
                a = None
                for c in range(2):
                    a = act.do(activation_(w, vn[:, b, 512 * c:512 * c + 512], ACT.Square,
                                                      accum_out=ss[:, b, c:c + 1]), t_vn[b], f, a)
                pf.give(j, [a])
                rv.append(a)
            a = dve.do(tensor_tensor_(ss[:, :, 2:3], ss[:, :, 0:1], ss[:, :, 1:2], ALU.add), rv)
            act.do(preload_act_table_set_(LN_SET), inc=False)
            a = rsqrt(ss[:, :, 4:5], ss[:, :, 2:3], ss[:, :, 3:4], 1.0 / 1024, a)
            act.do(preload_act_table_set_(EXP_SET), inc=False)
            rv = [dve.do(tensor_scalar_(vn[:, b, :], vn[:, b, :], ss[:, b, 4:5], None, ALU.mult), a)
                  for b in range(2)]
            yield
            for hh in range(8):
                while hh not in t_gb:
                    yield
                n, bk, fr = sideb.take()
                for b in range(2):
                    m = pe.do(matmul_(bk[:, 128 * b:128 * b + 128], vn[:, b, 128 * hh:128 * hh + 128],
                                                 wT[:, hh, :], start=True, stop=True), rv, t_wT, fr, inc=b == 1)
                i, v, f = vt.take()
                vv = v[:, 0:256].rearrange("p (a c) -> p a c", a=2)
                a = dve.do(scalar_tensor_tensor_(
                    vv, bk[:, 0:256].rearrange("p (a c) -> p a c", a=2), par_("sgu_g", hh),
                    bc(bS[:, hh, :], [[0, 2], [1, 128]]), ALU.mult, ALU.add), m, f, t_bS)
                sideb.give(n, [a])
                a = dve.do(tensor_tensor_(v[:, 0:256], v[:, 0:256], gb[:, hh, :], ALU.mult), a, t_gb[hh])
                t_yb[hh] = hilo((B1h[:, hh, :], B1l[:, hh, :]), v[:, 0:256], a, b1_free2)
                vt.give(i, t_yb[hh])
                yield

        side.append(sgu())
        run_t("even_in", 1024, 2048, X, xt_, ev_u, n1=256)
        run_t("even_in", 4096, 5120, X, xt_, ev_gb, n1=256)
        gate0 = lambda j: adaT[:, 0, 16 + j:17 + j]
        run_t("even_out", 0, 1024, (B0h, B0l), t_ya, ev_add(gate=gate0), n1=256)
        drain()
        b_free[0] = [(pe.sem, pe.n)]
        st = summed()
        run_t("even_out", 0, 1024, (B1h, B1l), t_yb, ev_add(gate0, [st]), k0=8, n1=256)
        b_free[1] = [(pe.sem, pe.n)]
        ph3.close()

        barrier()
        pho = ExitStack()
        gc = sbt(pho, "gc", [128, 8, 256])
        gd = sbt(pho, "gd", [128, 8, 256])
        pgl = ExitStack()
        gq = sbt(pgl, "gq", [128, 4, 256])
        gk = sbt(pgl, "gk", [128, 4, 256])
        gv = sbt(pgl, "gv", [128, 2, 1024])
        glr = sbt(pgl, "glr", [16, 256])
        gw = sbt(pgl, "gw", [16, 512])
        A1 = sbt(pgl, "A1", [128, 4, 256])
        A2 = sbt(pgl, "A2", [128, 4, 256])
        A3 = sbt(pgl, "A3", [128, 4, 256])
        KI = sbt(pgl, "KI", [128, 4, 256])
        K2 = sbt(pgl, "K2", [128, 4, 128])
        K3 = sbt(pgl, "K3", [128, 4, 128])
        dl = sbt(pgl, "dl", [128, 4, 4])
        At = Ring([sbt(pgl, f"At{i}", [128, 384]) for i in range(2)])
        oG = [z[:, 2 * i:2 * i + 2, :].rearrange("p h c -> p (h c)") for z in (A2, A3) for i in range(2)]
        mark = [(q.sem, q.n) for q in (act, dve, pool, pe)]
        t_gw = load("gw", gw[:, :], gwd, mark)
        H = [t_h[k] for k in range(8)]
        after_pe.clear()
        trs = st.finish()
        feed_ahead()
        xt_ = apply(h, H, 256, 16, trs, lambda k: G1[:, 1, k:k + 1], lambda k: adaT[:, 1, k:k + 1], X,
                    [(pe.sem, pe.n)] + ada_ready(1))
        t_gq, t_gk, t_gc, t_gd, t_gv = {}, {}, {}, {}, {}

        def ev_scaled(dst, toks, scale):
            def ev(j, ps, tok):
                toks[j] = act.do(mul_(dst[:, j, :], ps[:, 0:256], scale), tok)
                return [toks[j]]
            return ev

        def ev_qk(j, ps, tok):
            return ev_scaled(gq, t_gq, 128 ** -0.5)(j, ps, tok) if j < 4 else \
                ev_scaled(gk, t_gk, 1.0)(j - 4, ps, tok)

        t_glr = []

        def ev_glr(j, ps, tok):
            t_glr.append(act.do(copy_(glr[:, :], ps[0:16, 0:256]), tok))
            return [t_glr[0]]

        def ev_gv(b, c, ps, tok):
            t = act.do(copy_(gv[:, b, c:c + 256], ps[:, 0:256]), tok)
            t_gv.setdefault(c, []).append(t)
            return [t]

        flat = lambda x: x[:, :, :].rearrange("p h c -> p (h c)")
        c4 = lambda x: x[:, :, :].rearrange("p h (c t) -> p (h c) t", t=64)

        def gla():
            tz = []
            for g in range(2):
                n, bk, fr = sideb.take()
                for j in range(2):
                    hh = 2 * g + j
                    m = pe.do(matmul_(bk[:, 256 * j:256 * j + 256], gw[:, 128 * hh:128 * hh + 128],
                                                 glr[:, :], start=True, stop=True), t_glr, t_gw, fr)
                for j in range(2):
                    hh = 2 * g + j
                    a = act.do(activation_(A1[:, hh, :], bk[:, 256 * j:256 * j + 256], ACT.Identity,
                                                      bias=par_("gate_b", hh)), m, t_par)
                    tz.append(a)
                sideb.give(n, [a])
            yield
            a = act.do(activation_(flat(A2), flat(A1), ACT.Abs), tz)
            act.do(preload_act_table_set_(LN_SET), inc=False)
            a = act.do(activation_(flat(A2), flat(A2), ACT.Exp, scale=-1.0), a)
            a = act.do(activation_(flat(A2), flat(A2), ACT.Ln, bias=1.0), a)
            act.do(preload_act_table_set_(EXP_SET), inc=False)
            la = dve.do(scalar_tensor_tensor_(flat(A2), flat(A1), 0.0, flat(A2), ALU.min, ALU.subtract), a)
            yield
            yield
            a2, a3 = c4(A2), c4(A3)
            t = []
            for c in range(16):
                t.append(dve.do(tensor_tensor_scan_(a3[:, c, :], cst_("ones", 64), a2[:, c, :], 0.0,
                                                               ALU.mult, ALU.add), la))
            ends = bass.AP(A3[:, :, :].tensor, a3[:, :, 63:64].offset, [list(A3[:, :, :].ap[0]), [64, 16], [0, 64]])
            ep = act.do(activation_(flat(A1), flat(A3), ACT.Exp, scale=1.0 / 16), t)
            tdl = act.do(activation_(dl[:, :, :].rearrange("p h c -> p (h c)"),
                                                a3[:, :, 63:64].rearrange("p c o -> p (c o)"), ACT.Exp,
                                                scale=1.0 / 16), t)
            tq = dve.do(tensor_tensor_(flat(gq), flat(gq), flat(A1), ALU.mult), ep,
                        [t_gq[k] for k in range(4)])
            yield
            en = act.do(activation_(flat(A1), flat(A3), ACT.Exp, scale=-1.0 / 16), tq)
            tk = dve.do(tensor_tensor_(flat(KI), flat(gk), flat(A1), ALU.mult), en,
                        [t_gk[k] for k in range(4)])
            d = dve.do(tensor_tensor_(a2, ends, a3, ALU.subtract), t)
            d = act.do(activation_(flat(A2), flat(A2), ACT.Exp, scale=1.0 / 16), d)
            te = dve.do(tensor_tensor_(flat(gk), flat(gk), flat(A2), ALU.mult), d, tk)
            yield
            yield
            dlb = lambda i: bass.AP(dl[:, :, :].tensor, dl[:, :, i:i + 1].offset,
                                    [list(dl[:, :, :].ap[0]), [4, 4], [0, 64 if i == 1 else 128]])
            t2 = [pool.do(tensor_tensor_(K2[:, :, 0:64], gk[:, :, 0:64], dlb(1), ALU.mult), te, tdl),
                  pool.do(tensor_copy_(K2[:, :, 64:128], gk[:, :, 64:128]), te)]
            t3 = pool.do(tensor_tensor_(K3[:, :, :], K2[:, :, :], dlb(2), ALU.mult), t2)
            for i in range(2):
                z = [pool.do(memset_(At.bufs[i][:, 0:64], 0.0)),
                     pool.do(memset_(At.bufs[i][:, 256:320], 0.0))]
                At.free[i] = z
            yield
            yield
            ssb, oT = [], []
            sstok = []
            for hh in range(4):
                n, bk, fr = sideb.take()
                mm = lambda dst, l, r, inc: pe.do(matmul_(dst, l, r, start=True, stop=True), tq, tk, te, t2,
                                                  t3, fr, inc=inc)
                for c in range(4):
                    po = 64 * (c % 2)
                    co = 64 * (c // 2)
                    mm(bk[po:po + 64, co:co + 64], KI[:, hh, 64 * c:64 * c + 64], gq[:, hh, 64 * c:64 * c + 64], False)
                mm(bk[0:64, 128:192], gk[:, hh, 0:64], gq[:, hh, 64:128], False)
                mm(bk[0:64, 192:256], gk[:, hh, 128:192], gq[:, hh, 192:256], False)
                mm(bk[:, 256:320], K2[:, hh, :], gq[:, hh, 128:192], False)
                m = mm(bk[:, 320:384], K3[:, hh, :], gq[:, hh, 192:256], True)
                i, A, f = At.take()
                r = []
                for po in (0, 64):
                    c0 = po // 64
                    dst = A[po:po + 64, :].rearrange("p (a c) -> p a c", c=64)[:, c0::4, :]
                    r.append(dve.do(tensor_tensor_(
                        dst, bk[po:po + 64, 0:128].rearrange("p (a c) -> p a c", c=64),
                        bc(cst_("m64")[po:po + 64, :], [[0, 2], [1, 64]]), ALU.mult), m, f, t_cst))
                dst = A[0:64, :].rearrange("p (a c) -> p a c", c=64)[:, 1::4, :]
                r.append(dve.do(tensor_copy_(dst, bk[0:64, 128:256].rearrange("p (a c) -> p a c", c=64)),
                                m))
                r.append(dve.do(tensor_copy_(A[:, 128:256], bk[:, 256:384]), m))
                sideb.give(n, [r[-1]])
                yield
                n, bk, fr = sideb.take()
                for v in range(2):
                    vs = slice(256 * hh + 128 * v, 256 * hh + 128 * v + 128)
                    pe.do(matmul_(bk[:, 256 * v:256 * v + 256], gv[:, 0, vs], A[:, 0:256], start=True,
                                             stop=False), r, t_gv[256 * hh], fr, inc=False)
                    m = pe.do(matmul_(bk[:, 256 * v + 128:256 * v + 256], gv[:, 1, vs], A[:, 256:384],
                                                 start=False, stop=True), inc=v == 1)
                At.give(i, [m])
                a = dve.do(tensor_copy_(oG[hh], bk[:, :]), m)
                sideb.give(n, [a])
                oT.append(a)
                yield
                if hh % 2 == 0:
                    ssb.append(sideb.take())
                n, bk, fr = ssb[-1]
                for v in range(2):
                    i, s, f = sq.take()
                    a = act.do(activation_(s[:, 0:256], oG[hh][:, 256 * v:256 * v + 256], ACT.Square),
                               oT[hh], f)
                    m = pe.do(matmul_(bk[:, 256 * (hh % 2):256 * (hh % 2) + 256], cst_("ones"),
                                                 s[:, 0:256], start=v == 0, stop=v == 1), a, fr)
                    sq.give(i, [m])
                sstok.append(m)
                yield
            act.do(preload_act_table_set_(LN_SET), inc=False)
            tr = []
            for r in range(2):
                n, bk, _ = ssb[r]
                v = A1[:, 2 * r:2 * r + 2, :].rearrange("p h c -> p (h c)")
                t = rsqrt(v, bk[:, :], v, 1.0 / 256, sstok[2 * r + 1], tk)
                sideb.give(n, [t])
                tr.append(t)
            act.do(preload_act_table_set_(EXP_SET), inc=False)
            yield
            for hh in range(4):
                for v in range(2):
                    j = 2 * hh + v
                    o = oG[hh][:, 256 * v:256 * v + 256]
                    while j not in t_gc:
                        yield
                    a = dve.do(tensor_tensor_(o, o, A1[:, hh, :], ALU.mult), tr[hh // 2], oT[hh],
                               sstok[hh])
                    a = dve.do(scalar_tensor_tensor_(o, o, hp[:, 12 + j:13 + j], gc[:, j, :], ALU.mult,
                                                                ALU.mult), a, t_gc[j], t_hp)
                    t_ya[j] = hilo((B0h[:, j, :], B0l[:, j, :]), o, a, b_free[0])
                yield

        t_ya = {}
        t_yb = {}
        run_t("odd_in", 0, 1024, X, xt_, ev_qk, n1=256)
        run_t("odd_in", 2048, 2176, X, xt_, ev_glr, n1=256, w=128)
        side.append(gla())
        run_n("odd_in", 1024, 2048, X, xt_, (0, 128), ev_gv)

        def ev_gates(j, ps, tok):
            return ev_silu2(gc, t_gc)(j, ps, tok) if j < 8 else ev_silu2(gd, t_gd)(j - 8, ps, tok)

        run_t("odd_in", 5136, 7184, X, xt_, ev_gates, n1=256)
        drain()
        pgl.close()
        barrier()
        psb = ExitStack()
        kqv = Ring([tuple(sbt(psb, f"{n}{i}", [128, 2, 256]) for n in ("sq_", "sk_", "sv_")) for i in range(3)])
        zs = Ring([sbt(psb, f"zs{i}", [128, 384]) for i in range(3)])
        sl = Ring([sbt(psb, f"sl{i}", [128, 384]) for i in range(3)])
        act.do(preload_act_table_set_(LN_SET), inc=False)
        pair_use = {}

        def breaking(hh, bufs, tq, tk, tv, ip):
            j = hh % 2
            qq, kk, vv = bufs
            n, bk, fr = sideb.take()
            pe.do(matmul_(bk[:, 0:256], kk[:, j, 0:128], qq[:, j, :], start=True, stop=True), tq[j], tk[j],
                  fr, inc=False)
            m = pe.do(matmul_(bk[:, 256:384], kk[:, j, 128:256], qq[:, j, 128:256], start=True, stop=True))
            iz, z, fz = zs.take()
            il, l, fl = sl.take()
            a = act.do(copy_(z[:, :], bk[:, 0:384]), m, fz)
            sideb.give(n, [a])
            b = act.do(activation_(l[:, :], z[:, :], ACT.Abs), a, fl)
            b = act.do(activation_(l[:, :], l[:, :], ACT.Exp, scale=-1.0), b)
            b = act.do(activation_(l[:, :], l[:, :], ACT.Ln, bias=1.0), b)
            b = dve.do(scalar_tensor_tensor_(l[:, :], z[:, :], 0.0, l[:, :], ALU.max, ALU.add), b)
            dg = l[:, :].rearrange("p (a c) -> p a c", c=128)[:, 0::2, :]
            b = dve.do(tensor_tensor_(dg, dg, bc(cst_("strict"), [[0, 2], [1, 128]]), ALU.mult), b, t_cst)
            yield
            n, bk, fr = sideb.take()
            pe.do(matmul_(bk[:, 0:384], cst_("neguc"), l[:, :], start=True, stop=False), b, fr, inc=False)
            m = pe.do(matmul_(bk[:, 128:256], cst_("negones"), l[:, 256:384], start=False, stop=True))
            sl.give(il, [m])
            a = dve.do(tensor_tensor_(z[:, :], bk[:, 0:384], z[:, :], ALU.add), m)
            sideb.give(n, [a])
            dz = z[:, :].rearrange("p (a c) -> p a c", c=128)[:, 0::2, :]
            a = dve.do(tensor_tensor_(dz, dz, bc(cst_("negsb"), [[0, 2], [1, 128]]), ALU.add), a)
            a = act.do(activation_(z[:, :], z[:, :], ACT.Exp), a)
            yield
            while not tv:
                yield
            n, bk, fr = sideb.take()
            pe.do(matmul_(bk[:, 0:256], vv[:, 0, 128 * j:128 * j + 128], z[:, 0:256], start=True,
                                     stop=False), a, tv, fr, inc=False)
            m = pe.do(matmul_(bk[:, 128:256], vv[:, 1, 128 * j:128 * j + 128], z[:, 256:384], start=False,
                                         stop=True))
            zs.give(iz, [m])
            if j == 1:
                kqv.give(ip, [m])
            i, v, f = vt.take()
            d = dve.do(scalar_tensor_tensor_(v[:, 0:256], bk[:, 0:256], 0.5, gd[:, hh, :], ALU.mult,
                                                        ALU.mult), m, f, t_gd[hh])
            sideb.give(n, [d])
            t_yb[hh] = hilo((B1h[:, hh, :], B1l[:, hh, :]), v[:, 0:256], d, b_free[1])
            vt.give(i, t_yb[hh])
            yield

        steps["n"] = 1
        for p in range(4):
            ip, bufs, fr = kqv.take()
            tq, tk, tv = {}, {}, []

            def ev_s(dst, toks, scale):
                def ev(j, ps, tok):
                    toks[j] = act.do(mul_(dst[:, j, :], ps[:, 0:256], scale), tok, fr)
                    return [toks[j]]
                return ev

            def ev_sv(b, c, ps, tok):
                t = act.do(copy_(bufs[2][:, b, :], ps[:, 0:256]), tok, fr)
                tv.append(t)
                return [t]

            run_t("odd_in", 2064 + 256 * p, 2320 + 256 * p, X, xt_, ev_s(bufs[0], tq, 128 ** -0.5), n1=256)
            run_t("odd_in", 3088 + 256 * p, 3344 + 256 * p, X, xt_, ev_s(bufs[1], tk, 1.0), n1=256)
            run_n("odd_in", 4112 + 256 * p, 4368 + 256 * p, X, xt_, (0, 128), ev_sv)
            side.append(in_turn(breaking(2 * p, bufs, tq, tk, tv, ip), breaking(2 * p + 1, bufs, tq, tk, tv, ip)))
        gate1 = lambda j: adaT[:, 1, 16 + j:17 + j]
        run_t("odd_out", 0, 1024, (B0h, B0l), t_ya, ev_add(gate=gate1), n1=256)
        drain()
        st = summed()
        run_t("odd_out", 0, 1024, (B1h, B1l), t_yb, ev_add(gate1, [st]), k0=8, n1=256)

        H = [t_h[k] for k in range(8)]
        after_pe.clear()
        trs = st.finish()
        s_out = sem("s_out")
        for g in range(4):
            t = [dve.do(scalar_tensor_tensor_(h[:, k, 16:272], h[:, k, 16:272], par_("final_g", k),
                                                         rsB[:, 0:256], ALU.mult, ALU.mult), trs, H[k])
                 for k in (2 * g, 2 * g + 1)]
            sp.do(dma_start_(out[:, 2 * g:2 * g + 2, :], h[:, 2 * g:2 * g + 2, 16:272]), t, inc=s_out)
        sp.wait([(s_out, 64)])
        assert unit_no[0] == len(items_m) and fed[0] == len(items)
        psb.close()
        pho.close()
        ph2.close()

        block = ctx.enter_context(nc.Block())

        @block.sync
        def _(e):
            sp.emit(e)

        @block.tensor
        def _(e):
            pe.emit(e)

        @block.scalar
        def _(e):
            act.emit(e)

        @block.vector
        def _(e):
            dve.emit(e)

        @block.gpsimd
        def _(e):
            pool.emit(e)


def constants():
    i = np.arange(128)
    c = {}
    c["ident"] = np.eye(128)
    c["ones"] = np.ones((128, 128))
    c["negones"] = -np.ones((128, 128))
    c["neguc"] = -(i[:, None] >= i[None, :]).astype(float)
    c["strict"] = (i[:, None] < i[None, :]).astype(float)
    c["negsb"] = np.where(i[:, None] < i[None, :], 0.0, -1e30)
    c["m64"] = (i[:, None] % 64 <= np.arange(64)[None, :]).astype(float)
    col, w = i[:, None] % 64, np.arange(64)[None, :]
    start = np.clip(col - 8, 0, 48)
    c["negwin"] = np.where((w >= start) & (w < start + 16), 0.0, -1e30)
    c["cinv"] = np.concatenate([np.broadcast_to(1.0 / np.minimum(np.arange(16) + 1, 2 << g), (128, 16))
                                for g in range(4)], axis=1)
    c["tril"] = (i[:, None] <= i[None, :]).astype(float)
    cst = np.concatenate([c[n] for n in CCOLS], axis=1).astype(np.float32)
    msk = np.zeros((128, 7, 128))
    for n in range(7):
        b = 1 << n
        msk[:, n, :] = (i[:, None] // (2 * b) == i[None, :] // (2 * b)) & (i[:, None] // b != i[None, :] // b)
    return cst, msk.reshape(128, 896).astype(np.float32)


def kernel(**inputs):
    import concourse.bacc as bacc
    from concourse.bass_utils import run_bass_kernel_spmd as run

    x = {k: np.asarray(v) for k, v in inputs.items()}
    mats = {"w_in": x["w_in"][0], "w_na_out": x["w_na_out"][0], "w_hg_out": x["w_hg_out"][0], "w_o": x["w_o"][0],
            "w_up": x["w_up"][0], "w_down": x["w_down"][0], "even_in": x["even_in_w_2"][0],
            "pool_w": x["pool_w_2"][0].reshape(1024, 256), "even_out": x["even_out_w_2"][0],
            "odd_in": x["odd_in_w_2"][0], "odd_out": x["odd_out_w_2"][0]}
    items = plan()
    ws = np.empty((len(items), 128, 1024), np.float32)
    for n, it in enumerate(items):
        if it[0] == "m":
            _, name, k, nk, c, w = it
            ws[n] = mats[name][128 * k:128 * (k + nk), c:c + w].reshape(nk, 128, w).transpose(1, 0, 2).reshape(128, -1)
        else:
            _, layer, g, k = it
            w = x["ada_w_2"][layer, 128 * k:128 * k + 256, 512 * g:512 * g + 512]
            ws[n] = w.reshape(2, 128, 512).transpose(1, 0, 2).reshape(128, -1)

    def cols(a):
        return a.reshape(-1, 128).T

    p = {"norm_mix": x["norm_mix"], "norm_mlp": x["norm_mlp"], "norm_final": x["norm_final"],
         "hg_norm": x["hg_norm"], "lb": x["hg_lb_logits"], "c": x["c_2"], "ada_b": x["ada_b_2"],
         "norm_g": x["norm_g_2"], "pool_scale": x["pool_scale_2"], "sgu_g": x["sgu_norm_g_2"],
         "gate_b": x["gla_gate_b_2"], "gla_g": x["gla_norm_g_2"], "final_g": x["final_g_2"]}
    par = np.concatenate([cols(p[n]) for n in PCOLS], axis=1)
    cst, msk = constants()
    tok = np.concatenate([x["meta_tokens"], x["x"][0]], axis=0)
    xt = tok.T.reshape(8, 128, 272).transpose(1, 0, 2)
    pp, e, w = np.arange(128)[:, None, None], np.arange(6)[None, :, None], np.arange(64)[None, None, :]
    dc = np.clip(w - pp % 64, -15, 15) + 15
    bias = x["na_rpb"][0][:, e - 2 - pp // 64 + 7, dc].transpose(1, 0, 2, 3).reshape(128, 8, 384)
    bs = np.broadcast_to(x["sgu_b_2"][0][None], (128, 8, 128))
    wt = x["sgu_w_2"][0].transpose(2, 0, 1)
    arrays = {"ws": ws, "par": par, "cst": cst, "msk": msk, "xt": xt, "bias": bias, "gw": x["gla_gate_w_2"][0],
              "bs": bs, "wt": wt}
    arrays = {"in_" + k: np.ascontiguousarray(v) for k, v in arrays.items()}
    nc = bacc.Bacc("TRN2", target_bir_lowering=False, num_devices=1)
    args = [nc.dram_tensor(k, v.shape, mybir.dt.from_np(v.dtype), kind="ExternalInput").ap()
            for k, v in arrays.items()]
    out = nc.dram_tensor("out_0", (128, 8, 256), F32, kind="ExternalOutput").ap()
    build(nc, *args, out)
    r = run(nc, [arrays], core_ids=[0])
    y = np.asarray(r.results[0]["out_0"])
    return np.ascontiguousarray(y.transpose(1, 0, 2).reshape(1024, 256).T).reshape(1, 256, 1024)
```
